# Optimizing a Trainium2 kernel written in Bass

```python
import jax, jax.numpy as jnp
from jax import lax
import numpy as np

D_MODEL = 1024
BATCH = 1
SEQ = 256
DEPTH = 2

N_MIXERS = 4
RMS_EPS = 1e-6
LN_EPS = 1e-5

MLA_HEADS = 16
MLA_Q_RANK = 384
MLA_KV_RANK = 256
MLA_NOPE = 64
MLA_ROPE = 32
MLA_V = 64
ROPE_BASE = 10000.0
Q_BLOCK = 128

LRU_WIDTH = D_MODEL
LRU_HEADS = 8
LRU_HEAD_DIM = LRU_WIDTH // LRU_HEADS
CONV_WIDTH = 4
LRU_C = 8.0

POOL_WINDOWS = (2, 4, 8, 16)
POOL_GROUP = D_MODEL // len(POOL_WINDOWS)

GMLP_WIDTH = D_MODEL
GMLP_GROUPS = 4
GMLP_GROUP_DIM = GMLP_WIDTH // GMLP_GROUPS
GMLP_CHUNK = 128

D_FF = 3584
N_EXPERTS = 8
TOP_K = 2
MOE_BLOCK = 256

kernel_name = "hybrid_interleaved_mla_rglru_pool_gmlp_moe"

def _count(m, period):
    return len(range(m, DEPTH, period))

def rmsnorm(x, g):
    xf = x.astype(jnp.float32)
    y = xf * lax.rsqrt(jnp.mean(xf * xf, axis=-1, keepdims=True) + RMS_EPS)
    return (y * g.astype(jnp.float32)).astype(x.dtype)

def layernorm(x, g, b):
    xf = x.astype(jnp.float32)
    mu = jnp.mean(xf, axis=-1, keepdims=True)
    var = jnp.mean(jnp.square(xf - mu), axis=-1, keepdims=True)
    y = (xf - mu) * lax.rsqrt(var + LN_EPS)
    return (y * g.astype(jnp.float32) + b.astype(jnp.float32)).astype(x.dtype)

def apply_rope(x, cos, sin):
    half = x.shape[-1] // 2
    x1 = x[..., :half].astype(jnp.float32)
    x2 = x[..., half:].astype(jnp.float32)
    return jnp.concatenate([x1 * cos - x2 * sin, x2 * cos + x1 * sin], axis=-1).astype(x.dtype)

def mla_mixer(h, positions, w_in, q_norm, kv_norm, w_uq, w_ukv, w_o):
    B, S, _ = h.shape
    lat = h @ w_in
    c_q, c_kv, k_rope = jnp.split(lat, [MLA_Q_RANK, MLA_Q_RANK + MLA_KV_RANK], axis=-1)
    c_q = rmsnorm(c_q, q_norm)
    c_kv = rmsnorm(c_kv, kv_norm)
    q = (c_q @ w_uq).reshape(B, S, MLA_HEADS, MLA_NOPE + MLA_ROPE)
    q_nope, q_rope = q[..., :MLA_NOPE], q[..., MLA_NOPE:]
    kv = (c_kv @ w_ukv).reshape(B, S, MLA_HEADS, MLA_NOPE + MLA_V)
    k_nope, v = kv[..., :MLA_NOPE], kv[..., MLA_NOPE:]
    half = MLA_ROPE // 2
    inv_freq = ROPE_BASE ** (-jnp.arange(half, dtype=jnp.float32) / half)
    ang = positions.astype(jnp.float32)[..., None] * inv_freq
    cos, sin = jnp.cos(ang), jnp.sin(ang)
    q_rope = apply_rope(q_rope, cos[:, :, None, :], sin[:, :, None, :])
    k_rope = apply_rope(k_rope, cos, sin)
    scale = (MLA_NOPE + MLA_ROPE) ** -0.5
    nb = S // Q_BLOCK
    qn = q_nope.reshape(B, nb, Q_BLOCK, MLA_HEADS, MLA_NOPE).transpose(1, 0, 2, 3, 4)
    qr = q_rope.reshape(B, nb, Q_BLOCK, MLA_HEADS, MLA_ROPE).transpose(1, 0, 2, 3, 4)
    key_pos = jnp.arange(S)

    def block(args):
        qn_b, qr_b, b_idx = args
        s = (jnp.einsum('bqhd,bkhd->bhqk', qn_b, k_nope)
             + jnp.einsum('bqhr,bkr->bhqk', qr_b, k_rope)).astype(jnp.float32) * scale
        q_pos = b_idx * Q_BLOCK + jnp.arange(Q_BLOCK)
        mask = key_pos[None, :] <= q_pos[:, None]
        s = jnp.where(mask, s, -jnp.inf)
        p = jax.nn.softmax(s, axis=-1).astype(v.dtype)
        return jnp.einsum('bhqk,bkhd->bqhd', p, v)

    o = lax.map(block, (qn, qr, jnp.arange(nb)))
    o = o.transpose(1, 0, 2, 3, 4).reshape(B, S, MLA_HEADS * MLA_V)
    return o @ w_o

def rglru_mixer(h, w_in, conv_w, conv_b, w_a, b_a, w_x, b_x, lam, w_out):
    B, S, _ = h.shape
    gate_br, x_br = jnp.split(h @ w_in, 2, axis=-1)
    gate_br = jax.nn.gelu(gate_br)
    xc = lax.conv_general_dilated(
        x_br, conv_w.reshape(CONV_WIDTH, 1, LRU_WIDTH).astype(x_br.dtype),
        window_strides=(1,), padding=[(CONV_WIDTH - 1, 0)],
        dimension_numbers=('NWC', 'WIO', 'NWC'), feature_group_count=LRU_WIDTH) + conv_b
    xh = xc.reshape(B, S, LRU_HEADS, LRU_HEAD_DIM)
    r = jax.nn.sigmoid((jnp.einsum('bshi,hij->bshj', xh, w_a).reshape(B, S, LRU_WIDTH) + b_a).astype(jnp.float32))
    i_g = jax.nn.sigmoid((jnp.einsum('bshi,hij->bshj', xh, w_x).reshape(B, S, LRU_WIDTH) + b_x).astype(jnp.float32))
    log_a = -LRU_C * r * jax.nn.softplus(-lam.astype(jnp.float32))
    a = jnp.exp(log_a)
    mult = jnp.sqrt(-jnp.expm1(2.0 * log_a))
    b = mult * (i_g * xc.astype(jnp.float32))

    def combine(left, right):
        a_l, b_l = left
        a_r, b_r = right
        return a_l * a_r, a_r * b_l + b_r

    _, hs = lax.associative_scan(combine, (a, b), axis=1)
    y = hs.astype(h.dtype) * gate_br
    return y @ w_out

def pool_mixer(h, w_grp, scale):
    B, S, D = h.shape
    hf = h.astype(jnp.float32)
    cs = jnp.pad(jnp.cumsum(hf, axis=1), ((0, 0), (1, 0), (0, 0)))
    t = jnp.arange(S)
    groups = []
    for g, w in enumerate(POOL_WINDOWS):
        c = cs[..., g * POOL_GROUP:(g + 1) * POOL_GROUP]
        upper = c[:, 1:]
        lower = jnp.pad(c[:, :S + 1 - w], ((0, 0), (w - 1, 0), (0, 0)))
        count = jnp.minimum(t + 1, w).astype(jnp.float32)[None, :, None]
        groups.append((upper - lower) / count - hf[..., g * POOL_GROUP:(g + 1) * POOL_GROUP])
    pooled = jnp.stack(groups, axis=2).astype(h.dtype)
    out = jnp.einsum('bsgc,gcd->bsgd', pooled, w_grp).reshape(B, S, D)
    return out * scale

def gmlp_mixer(h, w_in, ln_g, ln_b, w_s, b_s, w_out):
    B, S, _ = h.shape
    z = jax.nn.gelu(h @ w_in)
    u, v = jnp.split(z, 2, axis=-1)
    v = layernorm(v, ln_g, ln_b)
    nc = S // GMLP_CHUNK
    vg = v.reshape(B, nc, GMLP_CHUNK, GMLP_GROUPS, GMLP_GROUP_DIM)
    causal = jnp.tril(jnp.ones((GMLP_CHUNK, GMLP_CHUNK), dtype=bool))
    ws = jnp.where(causal[None], w_s, jnp.zeros_like(w_s))
    v2 = jnp.einsum('gts,bnsgc->bntgc', ws, vg) + b_s.T[:, :, None]
    v2 = v2.reshape(B, S, GMLP_WIDTH)
    return (u * v2) @ w_out

def swiglu(h, w_gate, w_up, w_down):
    return (jax.nn.silu(h @ w_gate) * (h @ w_up)) @ w_down

def moe_swiglu(h, w_router, w_gate, w_up, w_down):
    B, S, D = h.shape
    T = B * S
    A = T * TOP_K
    xt = h.reshape(T, D)
    logits = (xt @ w_router).astype(jnp.float32)
    top_val, top_idx = lax.top_k(logits, TOP_K)
    gates = jax.nn.softmax(top_val, axis=-1)
    exp_flat = top_idx.reshape(A)
    tok_flat = jnp.arange(A, dtype=jnp.int32) // TOP_K
    gate_flat = gates.reshape(A)
    order = jnp.argsort(exp_flat)
    exp_sorted = exp_flat[order]
    tok_sorted = tok_flat[order]
    gate_sorted = gate_flat[order]
    sizes = jnp.bincount(exp_flat, length=N_EXPERTS)
    starts = jnp.cumsum(sizes) - sizes
    padded = (sizes + MOE_BLOCK - 1) // MOE_BLOCK * MOE_BLOCK
    pad_end = jnp.cumsum(padded)
    pad_start = pad_end - padded
    dest = pad_start[exp_sorted] + (jnp.arange(A) - starts[exp_sorted])
    n_blocks = -(-(A + N_EXPERTS * (MOE_BLOCK - 1)) // MOE_BLOCK)
    P = n_blocks * MOE_BLOCK
    buf = jnp.zeros((P, D), h.dtype).at[dest].set(xt[tok_sorted])
    block_start = jnp.arange(n_blocks) * MOE_BLOCK
    block_expert = jnp.minimum(jnp.sum(pad_end[None, :] <= block_start[:, None], axis=1), N_EXPERTS - 1)

    def expert_block(args):
        xb, e = args
        return swiglu(xb, w_gate[e], w_up[e], w_down[e])

    out = lax.map(expert_block, (buf.reshape(n_blocks, MOE_BLOCK, D), block_expert)).reshape(P, D)
    contrib = out[dest] * gate_sorted[:, None].astype(out.dtype)
    y = jnp.zeros((T, D), h.dtype).at[tok_sorted].add(contrib)
    return y.reshape(B, S, D)

def setup_inputs(seed: int = 0) -> dict:
    key = jax.random.key(seed)
    ks = iter(jax.random.split(key, 40))

    def nrm(shape, fan_in):
        return jax.random.normal(next(ks), shape, jnp.float32) * fan_in ** -0.5

    def gain(shape):
        return 1.0 + 0.02 * jax.random.normal(next(ks), shape, jnp.float32)

    def bias(shape):
        return 0.02 * jax.random.normal(next(ks), shape, jnp.float32)

    n_mla, n_lru, n_pool, n_gmlp = (_count(m, N_MIXERS) for m in range(N_MIXERS))
    n_dense, n_moe = _count(0, 2), _count(1, 2)
    D = D_MODEL
    x = jax.random.normal(next(ks), (BATCH, SEQ, D), jnp.float32)
    positions = jnp.broadcast_to(jnp.arange(SEQ, dtype=jnp.int32)[None, :], (BATCH, SEQ))
    inp = {
        "x": x,
        "positions": positions,
        "norm_mix": gain((DEPTH, D)),
        "norm_ffn": gain((DEPTH, D)),
        "norm_final": gain((D,)),
        "mla_w_in": nrm((n_mla, D, MLA_Q_RANK + MLA_KV_RANK + MLA_ROPE), D),
        "mla_q_norm": gain((n_mla, MLA_Q_RANK)),
        "mla_kv_norm": gain((n_mla, MLA_KV_RANK)),
        "mla_w_uq": nrm((n_mla, MLA_Q_RANK, MLA_HEADS * (MLA_NOPE + MLA_ROPE)), MLA_Q_RANK),
        "mla_w_ukv": nrm((n_mla, MLA_KV_RANK, MLA_HEADS * (MLA_NOPE + MLA_V)), MLA_KV_RANK),
        "mla_w_o": nrm((n_mla, MLA_HEADS * MLA_V, D), MLA_HEADS * MLA_V),
        "lru_w_in": nrm((n_lru, D, 2 * LRU_WIDTH), D),
        "lru_conv_w": nrm((n_lru, CONV_WIDTH, LRU_WIDTH), CONV_WIDTH),
        "lru_conv_b": bias((n_lru, LRU_WIDTH)),
        "lru_w_a": nrm((n_lru, LRU_HEADS, LRU_HEAD_DIM, LRU_HEAD_DIM), LRU_HEAD_DIM),
        "lru_b_a": bias((n_lru, LRU_WIDTH)),
        "lru_w_x": nrm((n_lru, LRU_HEADS, LRU_HEAD_DIM, LRU_HEAD_DIM), LRU_HEAD_DIM),
        "lru_b_x": bias((n_lru, LRU_WIDTH)),
    }
    u = jax.random.uniform(next(ks), (n_lru, LRU_WIDTH), jnp.float32, 0.9, 0.999)
    a0 = u ** (1.0 / LRU_C)
    inp["lru_lam"] = jnp.log(a0) - jnp.log1p(-a0)
    inp.update({
        "lru_w_out": nrm((n_lru, LRU_WIDTH, D), LRU_WIDTH),
        "pool_w_grp": nrm((n_pool, len(POOL_WINDOWS), POOL_GROUP, POOL_GROUP), POOL_GROUP),
        "pool_scale": gain((n_pool, D)),
        "gmlp_w_in": nrm((n_gmlp, D, 2 * GMLP_WIDTH), D),
        "gmlp_ln_g": gain((n_gmlp, GMLP_WIDTH)),
        "gmlp_ln_b": bias((n_gmlp, GMLP_WIDTH)),
        "gmlp_w_s": nrm((n_gmlp, GMLP_GROUPS, GMLP_CHUNK, GMLP_CHUNK), GMLP_CHUNK),
        "gmlp_b_s": gain((n_gmlp, GMLP_GROUPS, GMLP_CHUNK)),
        "gmlp_w_out": nrm((n_gmlp, GMLP_WIDTH, D), GMLP_WIDTH),
        "ffn_w_gate": nrm((n_dense, D, D_FF), D),
        "ffn_w_up": nrm((n_dense, D, D_FF), D),
        "ffn_w_down": nrm((n_dense, D_FF, D), D_FF),
        "moe_w_router": nrm((n_moe, D, N_EXPERTS), D),
        "moe_w_gate": nrm((n_moe, N_EXPERTS, D, D_FF), D),
        "moe_w_up": nrm((n_moe, N_EXPERTS, D, D_FF), D),
        "moe_w_down": nrm((n_moe, N_EXPERTS, D_FF, D), D_FF),
    })
    return inp

def reference(x, positions, norm_mix, norm_ffn, norm_final,
              mla_w_in, mla_q_norm, mla_kv_norm, mla_w_uq, mla_w_ukv, mla_w_o,
              lru_w_in, lru_conv_w, lru_conv_b, lru_w_a, lru_b_a, lru_w_x, lru_b_x, lru_lam, lru_w_out,
              pool_w_grp, pool_scale,
              gmlp_w_in, gmlp_ln_g, gmlp_ln_b, gmlp_w_s, gmlp_b_s, gmlp_w_out,
              ffn_w_gate, ffn_w_up, ffn_w_down,
              moe_w_router, moe_w_gate, moe_w_up, moe_w_down):
    h = x
    for i in range(DEPTH):
        m, j = i % N_MIXERS, i // N_MIXERS
        hn = rmsnorm(h, norm_mix[i])
        if m == 0:
            mix = mla_mixer(hn, positions, mla_w_in[j], mla_q_norm[j], mla_kv_norm[j],
                            mla_w_uq[j], mla_w_ukv[j], mla_w_o[j])
        elif m == 1:
            mix = rglru_mixer(hn, lru_w_in[j], lru_conv_w[j], lru_conv_b[j], lru_w_a[j], lru_b_a[j],
                              lru_w_x[j], lru_b_x[j], lru_lam[j], lru_w_out[j])
        elif m == 2:
            mix = pool_mixer(hn, pool_w_grp[j], pool_scale[j])
        else:
            mix = gmlp_mixer(hn, gmlp_w_in[j], gmlp_ln_g[j], gmlp_ln_b[j], gmlp_w_s[j],
                             gmlp_b_s[j], gmlp_w_out[j])
        h = h + mix
        hn = rmsnorm(h, norm_ffn[i])
        k = i // 2
        if i % 2 == 0:
            h = h + swiglu(hn, ffn_w_gate[k], ffn_w_up[k], ffn_w_down[k])
        else:
            h = h + moe_swiglu(hn, moe_w_router[k], moe_w_gate[k], moe_w_up[k], moe_w_down[k])
    return rmsnorm(h, norm_final)


_drawn_inputs = setup_inputs


def setup_inputs(seed=0):
    import zlib

    import numpy as np

    out = dict(_drawn_inputs(seed))
    spreads = {}
    factors = {'norm_final': 8.962, 'mla_q_norm': 8.0, 'lru_b_a': 26.805, 'lru_b_x': 15.789}
    for name, (base, spread) in spreads.items():
        noise = np.random.default_rng([zlib.crc32(name.encode()), seed]).standard_normal(out[name].shape)
        drawn = base * np.exp(spread * noise) if base else spread * noise
        out[name] = __import__('jax').numpy.asarray(drawn.astype(out[name].dtype))
    for name, factor in factors.items():
        out[name] = (out[name] * factor).astype(out[name].dtype)
    return out
```

```python
from contextlib import ExitStack

import numpy as np
import concourse.bass as bass
from concourse import mybir

F32 = mybir.dt.float32
F32R = mybir.dt.float32r
BF16 = mybir.dt.bfloat16
I32 = mybir.dt.int32
ALU = mybir.AluOpType
ACT = mybir.ActivationFunctionType
AX = mybir.AxisListType.X

P = 128
BANK = 512
BIG = 3.0e38
ROUND = 1.5 * 2.0 ** 23
RMS_EPS = 1e-6


def trunk(nc, x, positions, norm_mix, norm_ffn, norm_final, mla_w_in, mla_q_norm, mla_kv_norm,
          mla_w_uq, mla_w_ukv, mla_w_o, lru_w_in, lru_conv_w, lru_conv_b, lru_w_a, lru_b_a,
          lru_w_x, lru_b_x, lru_lam, lru_w_out, ffn_w_gate, ffn_w_up, ffn_w_down, moe_w_router,
          moe_w_gate, moe_w_up, moe_w_down, out):
    T, D = x.shape[1], x.shape[2]
    TT, KT = T // P, D // P
    QR, KVR = mla_q_norm.shape[1], mla_kv_norm.shape[1]
    LAT = mla_w_in.shape[2]
    ROPE = LAT - QR - KVR
    HALF = ROPE // 2
    HEADS, V = 16, 64
    NOPE = V
    QK = NOPE + ROPE
    SCALE = float(QK) ** -0.5
    F = ffn_w_gate.shape[2]
    E = moe_w_router.shape[2]
    STEPS = F // BANK
    SLOT_TOKENS = P
    SLOTS = 6
    UNIT = 2048
    CONV = lru_conv_w.shape[1]
    assert T == 256 and D == 1024 and F % BANK == 0 and LAT == 672

    with ExitStack() as ctx:
        def sb(stack, name, shape, dt):
            return stack.enter_context(nc.sbuf_tensor(name, shape, dt))

        def sem(name):
            return ctx.enter_context(nc.semaphore(name))

        raw = sb(ctx, "raw", [P, SLOTS, UNIT], F32)
        w_hi = sb(ctx, "w_hi", [P, SLOTS, UNIT], F32R)
        w_lo = sb(ctx, "w_lo", [P, SLOTS, UNIT], F32R)
        res = sb(ctx, "res", [P, TT, D], F32)
        ident = sb(ctx, "ident", [P, P], F32)
        pos_col = sb(ctx, "pos_col", [P, TT], F32)
        par = sb(ctx, "par", [P, 64], F32)
        inv_freq = sb(ctx, "inv_freq", [P, HALF], F32)
        ang = sb(ctx, "ang", [P, TT, HALF], F32)
        trig = sb(ctx, "trig", [P, 2, TT, HALF], F32)
        sumsq = sb(ctx, "sumsq", [P, 4], F32)
        rstd = sb(ctx, "rstd", [P, 4], F32)
        half = sb(ctx, "half", [P, 1], F32)
        zeros = sb(ctx, "zeros", [P, P], BF16)
        n_pass_i = sb(ctx, "n_pass_i", [1, 1], I32)
        neg_b = sb(ctx, "neg_b", [P, 2 * KT], F32)
        psum = ctx.enter_context(nc.psum_tensor("psum", [P, 8, BANK], F32))

        with ExitStack() as s:
            gain_mla = sb(s, "gain_mla", [P, D], F32)
            xn_mla = sb(s, "xn_mla", [P, TT, D], F32)
            xTh_mla = sb(s, "xTh_mla", [P, KT, T], F32R)
            xTl_mla = sb(s, "xTl_mla", [P, KT, T], F32R)
            q = sb(s, "q", [P, TT, HEADS, QK], F32)
            k = sb(s, "k", [P, TT, HEADS, QK], F32)
            mask = sb(s, "mask", [P, 2 * P], F32)
        with ExitStack() as s:
            gain_ffn = sb(s, "gain_ffn", [P, D], F32)
            xn_ffn = sb(s, "xn_ffn", [P, TT, D], F32)
            xTh_ffn = sb(s, "xTh_ffn", [P, KT, T], F32R)
            xTl_ffn = sb(s, "xTl_ffn", [P, KT, T], F32R)
            hid_f = sb(s, "hid_f", [P, TT, BANK], F32)
            hTh_f = sb(s, "hTh_f", [P, TT, 4, P], F32R)
            hTl_f = sb(s, "hTl_f", [P, TT, 4, P], F32R)
        with ExitStack() as s:
            gain_lru = sb(s, "gain_lru", [P, 2 * D], F32)
            xn_lru = sb(s, "xn_lru", [P, TT, D], F32)
            xTh_lru = sb(s, "xTh_lru", [P, KT, T], F32R)
            xTl_lru = sb(s, "xTl_lru", [P, KT, T], F32R)
            gate_br = sb(s, "gate_br", [P, KT, T], F32)
            x_br = sb(s, "x_br", [P, KT, CONV - 1 + T], F32)
            xc = sb(s, "xc", [P, 2, T], F32)
            xch = sb(s, "xch", [P, T], F32R)
            xcl = sb(s, "xcl", [P, T], F32R)
            a_sq = sb(s, "a_sq", [P, T], F32)
            sp_t = sb(s, "sp_t", [P, 8, KT], F32)
        with ExitStack() as s:
            xTh_moe = sb(s, "xTh_moe", [P, KT, T], F32R)
            xTl_moe = sb(s, "xTl_moe", [P, KT, T], F32R)
            xn_hi = sb(s, "xn_hi", [P, TT, D], F32R)
            hid_m = sb(s, "hid_m", [P, BANK], F32)
            hTh_m = sb(s, "hTh_m", [P, 4, P], F32R)
            hTl_m = sb(s, "hTl_m", [P, 4, P], F32R)
            onehot = sb(s, "onehot", [P, TT, SLOT_TOKENS], F32R)
            onehot_T = sb(s, "onehot_T", [P, TT, P], F32R)
            before = sb(s, "before", [P, P], F32)
            ones = sb(s, "ones", [P, P], F32)
            slot_no = sb(s, "slot_no", [P, SLOT_TOKENS], F32)
            expert_no = sb(s, "expert_no", [P, TT, E], F32)
            wr = sb(s, "wr", [P, KT, E], F32)
            wr_hi = sb(s, "wr_hi", [P, KT, E], F32R)
            wr_lo = sb(s, "wr_lo", [P, KT, E], F32R)
            rt = sb(s, "rt", [P, 8, TT, E], F32)
            rs = sb(s, "rs", [P, 8, TT], F32)
            key = sb(s, "key", [P, TT, E + 1], F32)
            gates = sb(s, "gates", [P, TT, E + 1], F32)
            with ExitStack() as s2:
                gain_moe = sb(s2, "gain_moe", [P, D], F32)
                xn_moe = sb(s2, "xn_moe", [P, TT, D], F32)
            with ExitStack() as s2:
                y_hi = sb(s2, "y_hi", [P, D], F32R)
                y_lo = sb(s2, "y_lo", [P, D], F32R)
            with ExitStack() as s2:
                gain_out = sb(s2, "gain_out", [P, D], F32)
                xn_out = sb(s2, "xn_out", [P, TT, D], F32)

        latent = res[:, :, 0:LAT]
        c_hi, c_lo = xTh_mla, xTl_mla
        rows = k[:, 0].rearrange("p h c -> p (h c)")[:, 0:P]
        angle_area = q[:, 1].rearrange("p h c -> p (h c)")
        pos_area = q[0:TT, 0].rearrange("p h c -> p (h c)")
        pos_f, pos_i = pos_area[:, 0:P], pos_area[:, P:2 * P].bitcast(I32)
        turns = angle_area[:, 0:2 * TT * HALF].rearrange("p (n t c) -> p n t c", n=2, t=TT)
        red = angle_area[:, P:P + 2 * TT * HALF].rearrange("p (n t c) -> p n t c", n=2, t=TT)
        rope_area = res[:, 1, LAT:LAT + HEADS * HALF].rearrange("p (h c) -> p h c", c=HALF)
        qkT = gain_mla.rearrange("p (b n) -> p b n", b=2)
        v = xn_mla
        probs = res[:, 0, 0:6 * P].rearrange("p (b n) -> p b n", b=2)
        probs_T = res[:, 1, 0:6 * P].rearrange("p (b n) -> p b n", b=2)
        att = res[:, 0, 6 * P:8 * P].rearrange("p (a b) -> p a b", b=32)
        mx, nmx, tot, inv = att[:, 0], att[:, 1], att[:, 2], att[:, 3]
        Q_BANKS = [(4, 5, 6), (0, 1, 2)]
        KV_BANKS = [(3, 7, 4, 5), (6, 0, 1, 2)]
        decay = gain_lru.rearrange("p (c t) -> p c t", t=T)
        drive = x_br[:, :, CONV - 1:]
        states = xn_lru.rearrange("p a (c t) -> p (a c) t", t=T)
        xg_hi = xTh_moe[:, 0:4, :].rearrange("p a t -> p (a t)").rearrange("p (k t) -> p k t", t=P)
        xg_lo = xTh_moe[:, 4:8, :].rearrange("p a t -> p (a t)").rearrange("p (k t) -> p k t", t=P)
        xn_lo = xTl_moe.rearrange("p k t -> p (k t)").rearrange("p (a d) -> p a d", a=TT)

        landed = [sem(f"landed{n}") for n in range(SLOTS)]
        hi_done = [sem(f"hi_done{n}") for n in range(SLOTS)]
        lo_done = [sem(f"lo_done{n}") for n in range(SLOTS)]
        used = [sem(f"used{n}") for n in range(SLOTS)]
        FFN_BASE = 2
        LRU_BASE = FFN_BASE + STEPS
        MOE_BASE = [LRU_BASE + (13 - s + SLOTS - 1) // SLOTS for s in range(SLOTS)]

        def mla_use(n):
            return n % SLOTS, n // SLOTS + 1

        def lru_use(n):
            return n % SLOTS, LRU_BASE + n // SLOTS + 1

        x_in = [sem(f"x_in{t}") for t in range(TT)]
        x_again = sem("x_again")
        gain_lat = sem("gain_lat")
        wx_landed = sem("wx_landed")
        ffn_added = sem("ffn_added")
        lru_added = sem("lru_added")
        moe_over = sem("moe_over")
        pass_over = sem("pass_over")
        var_ready = sem("var_ready")
        rstd_ready = sem("rstd_ready")
        mult_in = sem("mult_in")
        mult_ready = sem("mult_ready")
        small_in = sem("small_in")
        gain_in = [sem(f"gain_in{n}") for n in range(6)]
        const = sem("const")
        moe_const = sem("moe_const")
        link_s = sem("link_s")
        xn_ready = sem("xn_ready")
        xT_ps = sem("xT_ps")
        xT_hi = sem("xT_hi")
        xT_lo = sem("xT_lo")
        rows_ps = sem("rows_ps")
        cols_ready = sem("cols_ready")
        angles = sem("angles")
        trig_ready = sem("trig_ready")
        lat_ps = sem("lat_ps")
        lat_ready = sem("lat_ready")
        c_ready = sem("c_ready")
        c_ps = sem("c_ps")
        c_hi_s = sem("c_hi_s")
        c_lo_s = sem("c_lo_s")
        q_ps = sem("q_ps")
        q_copied = sem("q_copied")
        kv_ps = sem("kv_ps")
        kv_copied_a = sem("kv_copied_a")
        kv_copied_v = sem("kv_copied_v")
        pool_link = sem("pool_link")
        qk_ready = sem("qk_ready")
        qkT_ps = sem("qkT_ps")
        qkT_ready = sem("qkT_ready")
        score_ps = sem("score_ps")
        max_ready = sem("max_ready")
        exp_ready = sem("exp_ready")
        probs_ready = sem("probs_ready")
        probsT_ps = sem("probsT_ps")
        probsT_ready = sem("probsT_ready")
        o_ps = sem("o_ps")
        o_hi = sem("o_hi")
        o_lo = sem("o_lo")
        heads_over = sem("heads_over")
        proj_ps = sem("proj_ps")
        fg_ps = sem("fg_ps")
        fu_ps = sem("fu_ps")
        f_tanh = sem("f_tanh")
        f_mid = sem("f_mid")
        f_hid = sem("f_hid")
        fT_ps = sem("fT_ps")
        fT_hi = sem("fT_hi")
        fT_lo = sem("fT_lo")
        pads = sem("pads")
        sp_exp = sem("sp_exp")
        sp_in = sem("sp_in")
        xbr_ps = sem("xbr_ps")
        xbr_copied = sem("xbr_copied")
        gate_ps = sem("gate_ps")
        gate_copied = sem("gate_copied")
        xc_ready = sem("xc_ready")
        xc_hi = sem("xc_hi")
        xc_lo = sem("xc_lo")
        ri_ps = sem("ri_ps")
        ri_exp = sem("ri_exp")
        log_a = sem("log_a")
        a_ready = sem("a_ready")
        state_ready = sem("state_ready")
        gelu_ready = sem("gelu_ready")
        y_ready = sem("y_ready")
        yT_hi = sem("yT_hi")
        yT_lo = sem("yT_lo")
        out_ps = sem("out_ps")
        xnh_ready = sem("xnh_ready")
        wr_in = sem("wr_in")
        wr_hi_s = sem("wr_hi_s")
        wr_lo_s = sem("wr_lo_s")
        logit_ps = sem("logit_ps")
        top_diff = sem("top_diff")
        top_exp = sem("top_exp")
        mask_ready = sem("mask_ready")
        rank_ps = sem("rank_ps")
        plan_ready = sem("plan_ready")
        onehot_ready = sem("onehot_ready")
        gather_ps = sem("gather_ps")
        xg_hi_s = sem("xg_hi_s")
        xg_lo_s = sem("xg_lo_s")
        ohT_ps = sem("ohT_ps")
        ohT_ready = sem("ohT_ready")
        mg_ps = sem("mg_ps")
        mu_ps = sem("mu_ps")
        m_tanh = sem("m_tanh")
        m_mid = sem("m_mid")
        m_hid = sem("m_hid")
        mT_ps = sem("mT_ps")
        mT_hi = sem("mT_hi")
        mT_lo = sem("mT_lo")
        y_hi_s = sem("y_hi_s")
        y_lo_s = sem("y_lo_s")
        comb_ps = sem("comb_ps")
        added = sem("added")
        out_ready = sem("out_ready")
        stored = sem("stored")

        def slab(w, c0, n):
            return w[:, c0:c0 + n].rearrange("(k p) f -> p k f", p=P)

        def row_tiles(w, k0, n):
            return w[k0 * P:(k0 + n) * P, :].rearrange("(k p) f -> p k f", p=P)

        W_IN, W_UQ, W_UKV, W_O = 0, 3, 6, 8
        UQ, UKV = mla_w_uq.shape[2], mla_w_ukv.shape[2]
        IN_TILES = [(0, 3), (3, 3), (6, 2)]
        mla_units = [row_tiles(mla_w_in[0], a, n) for a, n in IN_TILES]
        mla_units += [row_tiles(mla_w_uq[0], a, 1) for a in range(QR // P)]
        mla_units += [row_tiles(mla_w_ukv[0], a, 1) for a in range(KVR // P)]
        mla_units += [row_tiles(mla_w_o[0], 2 * a, 2) for a in range(4)]
        L_X, L_AX, L_G, L_OUT = 0, 4, 5, 9
        lru_units = [slab(lru_w_in[0], D + 256 * u, 256) for u in range(4)]
        lru_units += [None]
        lru_units += [slab(lru_w_in[0], 256 * u, 256) for u in range(4)]
        lru_units += [row_tiles(lru_w_out[0], 2 * a, 2) for a in range(4)]
        ffn_v = [ffn_w_gate.rearrange("e (h k p) (j f) -> e h j p k f", h=2, p=P, f=BANK),
                 ffn_w_up.rearrange("e (h k p) (j f) -> e h j p k f", h=2, p=P, f=BANK),
                 ffn_w_down.rearrange("e (j h r p) d -> e h j p r d", h=2, r=2, p=P)]
        moe_v = [moe_w_gate[0].rearrange("e (h k p) (j f) -> e h j p k f", h=2, p=P, f=BANK),
                 moe_w_up[0].rearrange("e (h k p) (j f) -> e h j p k f", h=2, p=P, f=BANK),
                 moe_w_down[0].rearrange("e (j h r p) d -> e h j p r d", h=2, r=2, p=P)]

        def unit(t, s, b):
            return t[:, s, 0:UNIT // b * b].rearrange("p (a b) -> p a b", b=b)

        def load(sp, use, src):
            s, n = use
            if not isinstance(n, int) or n > 1:
                sp.wait_ge(lo_done[s], n - 1)
            a, b = src.shape[1], src.shape[2]
            dst = raw[:, s, 0:a * b].rearrange("p (a b) -> p a b", b=b)
            sp.dma_start(dst, src).then_inc(landed[s], 16)

        def split_hi(act, use, width=UNIT):
            s, n = use
            act.wait_ge(landed[s], n * 16)
            if not isinstance(n, int) or n > 1:
                act.wait_ge(used[s], n - 1)
            act.activation(w_hi[:, s, 0:width], raw[:, s, 0:width], ACT.Copy).then_inc(hi_done[s], 1)

        def split_lo(eng, use, width=UNIT):
            s, n = use
            eng.wait_ge(hi_done[s], n)
            eng.tensor_tensor(w_lo[:, s, 0:width], raw[:, s, 0:width], w_hi[:, s, 0:width].bitcast(F32),
                              ALU.subtract).then_inc(lo_done[s], 1)

        def ready(pe, use):
            s, n = use
            pe.wait_ge(lo_done[s], n)

        def product(pe, out_ap, terms, start=True, stop=True, marks=()):
            marks = dict(marks)
            for n, (sh, sl, mh, ml) in enumerate(terms):
                first, last = start and n == 0, stop and n == len(terms) - 1
                lone = dict(skip_group_check=True) if not (start and stop) else {}
                pe.matmul(out_ap, sh, mh, start=first, stop=False, **lone)
                pe.matmul(out_ap, sh, ml, start=False, stop=False, **lone)
                mm = pe.matmul(out_ap, sl, mh, start=False, stop=last, **lone)
                if n in marks:
                    mm.then_inc(marks[n], 1)

        def transpose_tokens(pe, phase, src):
            for t in range(TT):
                pe.wait_ge(xn_ready, TT * phase + t + 1)
                for h in range(2):
                    for a in range(4):
                        kt = 4 * h + a
                        mm = pe.transpose(psum[:, 2 * t + h, a * P:(a + 1) * P],
                                          src[:, t, kt * P:(kt + 1) * P], ident[:])
                    mm.then_inc(xT_ps, 1)

        def xT_high(act, phase, dst):
            for t in range(TT):
                for h in range(2):
                    act.wait_ge(xT_ps, 4 * phase + 2 * t + h + 1)
                    act.activation(dst[:, 4 * h:4 * h + 4, t * P:(t + 1) * P],
                                   psum[:, 2 * t + h].rearrange("p (a b) -> p a b", b=P),
                                   ACT.Copy).then_inc(xT_hi, 1)

        def xT_low(dve, phase, dst, high):
            for t in range(TT):
                for h in range(2):
                    dve.wait_ge(xT_hi, 4 * phase + 2 * t + h + 1)
                    area = (slice(None), slice(4 * h, 4 * h + 4), slice(t * P, (t + 1) * P))
                    dve.tensor_tensor(dst[area], psum[:, 2 * t + h].rearrange("p (a b) -> p a b", b=P),
                                      high[area].bitcast(F32), ALU.subtract).then_inc(xT_lo, 1)

        block = ctx.enter_context(nc.Block())

        @block.sync
        def _(sp):
            for t in range(TT):
                sp.dma_start(res[:, t, :], x[0, t * P:(t + 1) * P, :]).then_inc(x_in[t], 16)
            for n in range(len(mla_units)):
                load(sp, mla_use(n), mla_units[n])
            sp.wait_ge(heads_over, 1)
            sp.dma_start(res[:], x[0].rearrange("(t p) d -> p t d", p=P)).then_inc(x_again, 16)
            with sp.Fori(0, STEPS) as i:
                for s in range(SLOTS):
                    load(sp, (s, i + FFN_BASE + 1), ffn_v[s // 2][0, s % 2, i])
            for n in range(len(lru_units)):
                s, c = lru_use(n)
                if n != L_AX:
                    load(sp, (s, c), lru_units[n])
                    continue
                sp.wait_ge(lo_done[s], c - 1)
                half = UNIT // 2
                sp.dma_start(raw[:, s, 0:half].rearrange("p (h j) -> p h j", j=P),
                             lru_w_a[0].rearrange("h i j -> i h j")).then_inc(landed[s], 16)
                sp.dma_start(raw[:, s, half:UNIT].rearrange("p (h j) -> p h j", j=P),
                             lru_w_x[0].rearrange("h i j -> i h j")).then_inc(wx_landed, 16)

            def moe_loads(e, j, step):
                for s in range(SLOTS):
                    load(sp, (s, step + (MOE_BASE[s] + 1)), moe_v[s // 2][e, s % 2, j])

            with sp.Fori(0, E) as e:
                with sp.Fori(0, STEPS) as j:
                    moe_loads(e, j, e * STEPS + j)
            sp.wait_ge(plan_ready, 1)
            n_pass = sp.value_load(n_pass_i[0:1, 0:1], min_val=1, max_val=2)
            with sp.If(n_pass > 1):
                with sp.Fori(0, E) as e:
                    with sp.Fori(0, STEPS) as j:
                        moe_loads(e, j, e * STEPS + j + E * STEPS)
            for t in range(TT):
                sp.wait_ge(out_ready, t + 1)
                sp.dma_start(out[0, t * P:(t + 1) * P, :], xn_out[:, t, :]).then_inc(stored, 16)
            sp.wait_ge(stored, 16 * TT)

        @block.gpsimd
        def _(pool):
            links = [0]

            def link(ins):
                links[0] += 1
                ins.then_inc(pool_link, 1)
                pool.wait_ge(pool_link, links[0])

            def gain(n, dst, src):
                pool.dma_start(dst, src.partition_broadcast(P)).then_inc(gain_in[n], 16)

            gain(0, gain_mla[:], norm_mix[0])
            for n, w in enumerate([lru_conv_w[0].rearrange("w (c p) -> (w c) p", p=P)]
                                  + [a[0].rearrange("(c p) -> c p", p=P)
                                     for a in (lru_conv_b, lru_b_a, lru_b_x, lru_lam)]):
                at = 0 if n == 0 else 24 + 8 * n
                pool.dma_start(rows[at:at + w.shape[0], :], w).then_inc(small_in, 16)
            pool.dma_start(pos_i, positions[0].rearrange("(t p) -> t p", p=P)).then_inc(small_in, 16)
            link(pool.memset(ident[:], 0.0))
            link(pool.memset(mask[:], 0.0))
            pool.affine_select(out=ident[:], in_=ident[:], compare_op=ALU.not_equal, fill=1.0, base=0,
                               pattern=[[-1, P]], channel_multiplier=1).then_inc(const, 1)
            pool.affine_select(out=mask[:, P:2 * P], in_=mask[:, P:2 * P], compare_op=ALU.is_ge,
                               fill=-BIG, base=0, pattern=[[-1, P]], channel_multiplier=1).then_inc(const, 1)
            pool.memset(zeros[:], 0.0).then_inc(const, 1)
            link(pool.memset(half[:], -0.5))

            def inverse_roots(n, at=0, width=TT):
                pool.wait_ge(var_ready, n)
                r = rstd[:, at:at + width]
                pool.tensor_tensor(r, r, half[:, 0:1].broadcast_to([P, width]), ALU.pow).then_inc(rstd_ready, 1)

            inverse_roots(1)
            for n in range(HALF):
                f = float(np.float32(10000.0) ** np.float32(-n / HALF))
                pool.memset(inv_freq[:, n:n + 1], f).then_inc(const, 1)
            pool.wait_ge(xn_ready, TT)
            pool.dma_start(gain_mla[:, 0:QR], mla_q_norm[0].partition_broadcast(P)).then_inc(gain_in[1], 16)
            pool.dma_start(gain_mla[:, QR:QR + KVR], mla_kv_norm[0].partition_broadcast(P)).then_inc(gain_lat, 16)
            pool.wait_ge(trig_ready, 1)

            def rope(t, src, dst, width, areas):
                sin = trig[:, 0, t].unsqueeze(1).broadcast_to([P, width, HALF])
                cos = trig[:, 1, t].unsqueeze(1).broadcast_to([P, width, HALF])
                x1, x2 = src[:, :, 0:HALF], src[:, :, HALF:ROPE]
                a, b, c = areas
                pool.tensor_tensor(a, x1, cos, ALU.mult).then_inc(pool_link, 1)
                pool.tensor_tensor(b, x2, sin, ALU.mult).then_inc(pool_link, 1)
                links[0] += 2
                link(pool.tensor_tensor(c, x1, sin, ALU.mult))
                link(pool.tensor_tensor(dst[:, :, 0:HALF], a, b, ALU.subtract))
                link(pool.tensor_tensor(a, x2, cos, ALU.mult))
                link(pool.tensor_tensor(dst[:, :, HALF:ROPE], a, c, ALU.add))

            def areas(t, width):
                return [k[:, t, 0:width, NOPE + 16 * 0:NOPE + 16], k[:, t, 0:width, NOPE + 16:NOPE + 32],
                        rope_area[:, 0:width, :]]

            pool.wait_ge(lat_ready, 4)
            inverse_roots(2)
            inverse_roots(3, at=TT)
            for t in range(TT):
                kr = latent[:, t, QR + KVR:LAT].unsqueeze(1)
                rope(t, kr, kr, 1, areas(t, 1))
            for t in range(TT):
                pool.wait_ge(q_copied, 3 * (t + 1))
                qr = q[:, t, :, NOPE:QK]
                rope(t, qr, qr, HEADS, areas(t, HEADS))
                pool.tensor_copy(k[:, t, :, NOPE:QK],
                                 latent[:, t, QR + KVR:LAT].unsqueeze(1).broadcast_to([P, HEADS, ROPE])
                                 ).then_inc(qk_ready, 1)
            pool.wait_ge(heads_over, 1)
            gain(2, gain_ffn[:], norm_ffn[0])
            inverse_roots(4)
            with pool.Fori(0, STEPS) as i:
                split_lo(pool, (SLOTS - 1, i + FFN_BASE + 1))
            pool.wait_ge(xn_ready, 2 * TT)
            gain(3, gain_lru[:, 0:D], norm_mix[1])
            pool.wait_ge(ffn_added, 1)
            pool.memset(x_br[:, :, 0:CONV - 1], 0.0).then_inc(pads, 1)
            inverse_roots(5)
            pool.wait_ge(yT_lo, 2)
            pool.wait_ge(lru_added, 1)
            gain(4, gain_moe[:], norm_ffn[1])
            pool.dma_start(wr[:], moe_w_router[0].rearrange("(k p) e -> p k e", p=P)).then_inc(wr_in, 16)
            pool.memset(ones[:], 1.0).then_inc(moe_const, 1)
            pool.memset(before[:], 1.0).then_inc(moe_const, 1)
            pool.wait_ge(moe_const, 2)
            pool.affine_select(out=before[:], in_=before[:], compare_op=ALU.is_gt, fill=0.0, base=0,
                               pattern=[[1, P]], channel_multiplier=-1).then_inc(moe_const, 1)
            pool.iota(slot_no[:], pattern=[[1, SLOT_TOKENS]], base=0, channel_multiplier=0,
                      allow_small_or_imprecise_dtypes=True).then_inc(moe_const, 1)
            pool.iota(expert_no[:], pattern=[[0, TT], [1, E]], base=0, channel_multiplier=0,
                      allow_small_or_imprecise_dtypes=True).then_inc(moe_const, 1)
            pool.memset(key[:], -1.0).then_inc(moe_const, 1)
            inverse_roots(6)
            pool.wait_ge(plan_ready, 1)
            n_pass = pool.value_load(n_pass_i[0:1, 0:1], min_val=1, max_val=2)

            def pool_use(s, step):
                return s, step + (MOE_BASE[s] + 1)

            with pool.Fori(0, n_pass) as p:
                split_lo(pool, pool_use(1, p * (E * STEPS)))
                with pool.Fori(0, E * STEPS - 1) as j:
                    split_lo(pool, pool_use(5, p * (E * STEPS) + j))
                    split_lo(pool, pool_use(1, p * (E * STEPS) + j + 1))
                split_lo(pool, pool_use(5, p * (E * STEPS) + (E * STEPS - 1)))
            pool.wait_ge(moe_over, 1)
            gain(5, gain_out[:], norm_final)
            inverse_roots(7)

        @block.scalar
        def _(act):
            def copy(dst, src):
                return act.activation(dst, src, ACT.Copy)

            for n in range(W_IN, W_UQ):
                split_hi(act, mla_use(n), IN_TILES[n][1] * LAT)
            xT_high(act, 0, xTh_mla)
            act.wait_ge(angles, 1)
            act.activation(trig[:], red[:], ACT.Sin).then_inc(trig_ready, 1)
            for n in range(W_UQ, W_UKV):
                split_hi(act, mla_use(n), UQ)
            for t in range(TT):
                for b, (c0, c1) in enumerate([(0, BANK), (BANK, LAT)]):
                    if t == TT - 1 and b == 1:
                        act.wait_ge(used[mla_use(W_UQ - 1)[0]], 1)
                    else:
                        act.wait_ge(lat_ps, 2 * t + b + 1)
                    copy(latent[:, t, c0:c1], psum[:, 4 + 2 * t + b, 0:c1 - c0]).then_inc(lat_ready, 1)
            for n in range(W_UKV, W_O):
                split_hi(act, mla_use(n), UKV)
            for t in range(TT):
                for b, n in enumerate([4, 1]):
                    act.wait_ge(c_ps, 2 * t + b + 1)
                    copy(c_hi[:, 4 * b:4 * b + n, t * P:(t + 1) * P],
                         psum[:, 2 * t + b, 0:n * P].rearrange("p (a b) -> p a b", b=P)).then_inc(c_hi_s, 1)
            for t in range(TT):
                for b in range(3):
                    if t == TT - 1 and b == 2:
                        act.wait_ge(used[mla_use(W_UKV - 1)[0]], mla_use(W_UKV - 1)[1])
                    else:
                        act.wait_ge(q_ps, 3 * t + b + 1)
                    copy(q[:, t].rearrange("p h c -> p (h c)")[:, b * BANK:(b + 1) * BANK],
                         psum[:, Q_BANKS[t][b]]).then_inc(q_copied, 1)
            for n in range(W_O, W_O + 2):
                split_hi(act, mla_use(n))
            for t in range(TT):
                for b in (0, 1):
                    act.wait_ge(kv_ps, 4 * t + b + 1)
                    src = psum[:, KV_BANKS[t][b]].rearrange("p (h c) -> p h c", h=4)
                    copy(k[:, t, 4 * b:4 * b + 4, 0:NOPE], src[:, :, 0:NOPE]).then_inc(kv_copied_a, 1)
                    copy(v[:, t, 4 * b * V:4 * (b + 1) * V].rearrange("p (h c) -> p h c", h=4),
                         src[:, :, NOPE:NOPE + V]).then_inc(kv_copied_a, 1)
            for n in range(W_O + 2, W_O + 4):
                split_hi(act, mla_use(n))

            def qk_copy(h):
                act.wait_ge(qkT_ps, h + 1)
                copy(qkT[0:QK, h % 2, :], psum[0:QK, h % 2, :]).then_inc(qkT_ready, 1)

            def exps(h):
                act.wait_ge(max_ready, h + 1)
                b = h % 2
                for r, (c0, c1) in enumerate([(0, P), (P, 3 * P)]):
                    act.activation(probs[:, b, c0:c1], probs[:, b, c0:c1], ACT.Exp, scale=SCALE,
                                   bias=nmx[:, 2 * b + r:2 * b + r + 1],
                                   accum_out=tot[:, 2 * b + r:2 * b + r + 1]).then_inc(exp_ready, 1)

            def pT_copy(h):
                act.wait_ge(probsT_ps, h + 1)
                copy(probs_T[:, h % 2, :], psum[:, 4 + h % 2, 0:3 * P]).then_inc(probsT_ready, 1)

            def o_high(g):
                act.wait_ge(o_ps, g + 1)
                copy(xTh_mla[:, g, :], psum[:, 6 + g % 2, 0:T]).then_inc(o_hi, 1)

            qk_copy(0)
            qk_copy(1)
            for h in range(HEADS + 3):
                if h < HEADS:
                    exps(h)
                if 1 <= h <= HEADS:
                    pT_copy(h - 1)
                if h + 2 < HEADS:
                    qk_copy(h + 2)
                if h >= 3 and h % 2 == 1 and (h - 3) // 2 < HEADS // 2:
                    o_high((h - 3) // 2)

            xT_high(act, 1, xTh_ffn)
            with act.Fori(0, STEPS) as i:
                for s in range(4):
                    split_hi(act, (s, i + FFN_BASE + 1))
                act.wait_ge(fg_ps, i + 1)
                act.activation(hid_f[:, 0], psum[:, 0], ACT.Tanh, scale=0.5).then_inc(f_tanh, 1)
                for s in range(4, 6):
                    split_hi(act, (s, i + FFN_BASE + 1))
                act.wait_ge(used[1], i + FFN_BASE + 1)
                act.activation(hid_f[:, 1], psum[:, 2], ACT.Tanh, scale=0.5).then_inc(f_tanh, 1)
                for t in range(TT):
                    act.wait_ge(fT_ps, i * TT + t + 1)
                    copy(hTh_f[:, t], psum[:, 2 * t].rearrange("p (a b) -> p a b", b=P)).then_inc(fT_hi, 1)

            for n in range(L_X, L_AX):
                split_hi(act, lru_use(n))
            xT_high(act, 2, xTh_lru)
            s_ax = lru_use(L_AX)
            act.wait_ge(wx_landed, 16)
            split_hi(act, s_ax)
            act.wait_ge(sp_in, 1)
            act.activation(sp_t[:, 0], sp_t[:, 1], ACT.Exp, scale=-1.0).then_inc(sp_exp, 1)
            split_hi(act, lru_use(L_G))
            for c in range(KT):
                s, n = lru_use(L_X + c // 2)
                if c % 2 == 0:
                    act.wait_ge(xbr_ps, c // 2 + 1)
                else:
                    act.wait_ge(used[s], n)
                copy(x_br[:, c, CONV - 1:], psum[:, c, 0:T]).then_inc(xbr_copied, 1)
                if c % 2 == 1 and c < 7:
                    split_hi(act, lru_use(L_G + 1 + c // 2))

            def xc_high(c):
                act.wait_ge(xc_ready, c + 1)
                if c > 0:
                    act.wait_ge(ri_ps, c)
                copy(xch[:], xc[:, c % 2]).then_inc(xc_hi, 1)

            def gate_exps(c):
                if c < KT - 1:
                    act.wait_ge(ri_ps, c + 1)
                else:
                    act.wait_ge(used[s_ax[0]], s_ax[1])
                for g, dst in enumerate([decay[:, c], drive[:, c]]):
                    act.activation(dst, psum[:, c % 4, g * T:(g + 1) * T], ACT.Exp,
                                   scale=-1.0, bias=neg_b[:, g * KT + c:g * KT + c + 1]).then_inc(ri_exp, 1)

            def decays(c):
                act.wait_ge(log_a, c + 1)
                act.activation(states[:, c], decay[:, c], ACT.Tanh, scale=-1.0).then_inc(a_ready, 1)
                act.activation(decay[:, c], decay[:, c], ACT.Exp).then_inc(a_ready, 1)

            def multipliers(h):
                act.wait_ge(mult_in, 4 * h + 4)
                act.activation(states[:, 4 * h:4 * h + 4], states[:, 4 * h:4 * h + 4],
                               ACT.Sqrt).then_inc(mult_ready, 1)

            def gate_copy(c):
                s, n = lru_use(L_G + c // 2)
                if c % 2 == 0:
                    act.wait_ge(gate_ps, c // 2 + 1)
                else:
                    act.wait_ge(used[s], n)
                copy(gate_br[:, c, :], psum[:, 4 + c % 4, 0:T]).then_inc(gate_copied, 1)

            xc_high(0)
            for c in range(KT):
                gate_copy(c)
                gate_exps(c)
                if c + 1 < KT:
                    xc_high(c + 1)
                if c > 0:
                    decays(c - 1)
                if c == 5:
                    multipliers(0)
                if c == 5:
                    split_hi(act, lru_use(L_OUT))
                if c == 6:
                    split_hi(act, lru_use(L_OUT + 2))
            decays(KT - 1)
            multipliers(1)
            act.activation(gate_br[:], gate_br[:], ACT.Gelu_apprx_tanh).then_inc(gelu_ready, 1)
            split_hi(act, lru_use(L_OUT + 1))
            for h in range(2):
                act.wait_ge(y_ready, h + 1)
                copy(xTh_lru[:, 4 * h:4 * h + 4, :], states[:, 4 * h:4 * h + 4, :]).then_inc(yT_hi, 1)
            split_hi(act, lru_use(L_OUT + 3))

            xT_high(act, 3, xTh_moe)
            for t in range(TT):
                copy(xn_hi[:, t], xn_moe[:, t]).then_inc(xnh_ready, 1)
            act.wait_ge(wr_in, 16)
            copy(wr_hi[:], wr[:]).then_inc(wr_hi_s, 1)
            act.wait_ge(top_diff, 1)
            act.activation(rs[:, 3], rs[:, 2], ACT.Exp).then_inc(top_exp, 1)
            act.wait_ge(plan_ready, 1)
            n_pass = act.value_load(n_pass_i[0:1, 0:1], min_val=1, max_val=2)

            def xg_high(n):
                for b in range(2):
                    act.wait_ge(gather_ps, n * 2 + (b - 1))
                    copy(xg_hi[:, 4 * b:4 * b + 4, :],
                         psum[:, 6 + b].rearrange("p (a b) -> p a b", b=P)).then_inc(xg_hi_s, 1)

            def onehot_T_copy(n):
                act.wait_ge(ohT_ps, n)
                copy(onehot_T[:], psum[:, 1, 256:512].rearrange("p (a b) -> p a b", b=P)).then_inc(ohT_ready, 1)

            def use(s, step):
                return s, step + (MOE_BASE[s] + 1)

            def step_work(step, more=True, first=None, last=None):
                if first is not None:
                    act.wait_ge(used[5], use(5, step)[1] - 1)
                    for b in range(2):
                        copy(y_hi[:, b * BANK:(b + 1) * BANK], psum[:, 4 + b]).then_inc(y_hi_s, 1)
                split_hi(act, use(4, step))
                act.wait_ge(mg_ps, step + 1)
                act.activation(hid_m[:, 0:256], psum[:, 0, 0:256], ACT.Tanh, scale=0.5).then_inc(m_tanh, 1)
                split_hi(act, use(5, step))
                act.wait_ge(used[1], use(1, step)[1])
                act.activation(hid_m[:, 256:512], psum[:, 2, 0:256], ACT.Tanh, scale=0.5).then_inc(m_tanh, 1)
                for b in range(2):
                    if b == 1 and more:
                        for s in (0, 1):
                            split_hi(act, use(s, step + 1))
                    act.wait_ge(mT_ps, step * 2 + (b + 1))
                    copy(hTh_m[:, 2 * b:2 * b + 2],
                         psum[:, 2 * b, 256:512].rearrange("p (a b) -> p a b", b=P)).then_inc(mT_hi, 1)
                if first is not None:
                    onehot_T_copy(first + 2)
                if last is not None:
                    xg_high(last + 2)
                if more:
                    for s in (2, 3):
                        split_hi(act, use(s, step + 1))

            def expert_work(p, e, more):
                step, count = p * (E * STEPS) + e * STEPS, p * (E + 1) + e
                step_work(step, first=count)
                with act.Fori(1, STEPS - 1) as j:
                    step_work(step + j)
                step_work(step + (STEPS - 1), more=more, last=count)

            with act.Fori(0, n_pass) as p:
                xg_high(p * (E + 1) + 1)
                onehot_T_copy(p * (E + 1) + 1)
                for s in range(4):
                    split_hi(act, use(s, p * (E * STEPS)))
                with act.Fori(0, E - 1) as e:
                    expert_work(p, e, True)
                expert_work(p, E - 1, False)
                act.wait_ge(used[5], use(5, p * (E * STEPS))[1] + (E * STEPS - 1))
                for b in range(2):
                    copy(y_hi[:, b * BANK:(b + 1) * BANK], psum[:, 4 + b]).then_inc(y_hi_s, 1)

        @block.tensor
        def _(pe):
            pe.wait_ge(const, 1)
            pe.wait_ge(cols_ready, 1)
            pe.transpose(psum[:, 4, 0:TT], pos_f, ident[0:TT, 0:TT]).then_inc(rows_ps, 1)
            pe.transpose(psum[:, 5, 0:64], rows[0:64, :], ident[0:64, 0:64]).then_inc(rows_ps, 1)
            transpose_tokens(pe, 0, xn_mla)

            pe.wait_ge(xT_lo, 4)
            pe.wait_ge(cols_ready, 3)
            for t in range(TT):
                for b, (c0, c1) in enumerate([(0, BANK), (BANK, LAT)]):
                    terms, marks = [], {}
                    last = t == TT - 1 and b == 1
                    for n, (k0, nk) in enumerate(IN_TILES):
                        if t == 0 and b == 0:
                            ready(pe, mla_use(n))
                        s = mla_use(n)[0]
                        for a in range(nk):
                            tok = slice(t * P, (t + 1) * P)
                            terms.append((xTh_mla[:, k0 + a, tok], xTl_mla[:, k0 + a, tok],
                                          unit(w_hi, s, LAT)[:, a, c0:c1], unit(w_lo, s, LAT)[:, a, c0:c1]))
                        if last:
                            marks[len(terms) - 1] = used[s]
                    if not last:
                        marks[len(terms) - 1] = lat_ps
                    product(pe, psum[:, 4 + 2 * t + b, 0:c1 - c0], terms, marks=marks)
            for t in range(TT):
                pe.wait_ge(c_ready, t + 1)
                for b, n in enumerate([4, 1]):
                    for a in range(n):
                        col = (4 * b + a) * P
                        mm = pe.transpose(psum[:, 2 * t + b, a * P:(a + 1) * P],
                                          latent[:, t, col:col + P], ident[:])
                    mm.then_inc(c_ps, 1)

            def up_projection(first, tiles, k0, banks, done):
                for t in range(TT):
                    pe.wait_ge(c_lo_s, 2 * (t + 1))
                    for b, bank in enumerate(banks[t]):
                        terms, marks = [], {}
                        last = t == TT - 1 and b == len(banks[t]) - 1
                        for a in range(tiles):
                            s = mla_use(first + a)[0]
                            if t == 0 and b == 0:
                                ready(pe, mla_use(first + a))
                            tok = slice(t * P, (t + 1) * P)
                            cols = slice(b * BANK, (b + 1) * BANK)
                            terms.append((c_hi[:, k0 + a, tok], c_lo[:, k0 + a, tok], w_hi[:, s, cols], w_lo[:, s, cols]))
                            if last:
                                marks[a] = used[s]
                        if not last:
                            marks[tiles - 1] = done
                        for sm, n in BANK_FREE.get((first, t, b), ()):
                            pe.wait_ge(sm, n)
                        product(pe, psum[:, bank], terms, marks=marks)

            BANK_FREE = {
                (W_UQ, 0, 0): [(lat_ready, 4)],
                (W_UQ, 1, 0): [(c_lo_s, 4)],
                (W_UKV, 0, 2): [(q_copied, 1)], (W_UKV, 0, 3): [(q_copied, 2)],
                (W_UKV, 1, 0): [(q_copied, 3)], (W_UKV, 1, 1): [(q_copied, 4)],
                (W_UKV, 1, 2): [(q_copied, 5)], (W_UKV, 1, 3): [(q_copied, 6)],
            }
            up_projection(W_UQ, QR // P, 0, Q_BANKS, q_ps)
            up_projection(W_UKV, KVR // P, QR // P, KV_BANKS, kv_ps)

            def transpose_qk(h):
                if h >= 2:
                    pe.wait_ge(qkT_ready, h - 1)
                for n, src in enumerate([q[:, 0, h], q[:, 1, h], k[:, 0, h], k[:, 1, h]]):
                    mm = pe.transpose(psum[0:QK, h % 2, n * P:(n + 1) * P], src, ident[:])
                mm.then_inc(qkT_ps, 1)

            def scores(h):
                pe.wait_ge(qkT_ready, h + 1)
                if h >= 2:
                    pe.wait_ge(max_ready, h - 1)
                s = qkT[0:QK, h % 2]
                pe.matmul(psum[:, 2 + h % 2, 0:P], s[:, 0:P], s[:, 2 * P:3 * P], start=True, stop=True)
                pe.matmul(psum[:, 2 + h % 2, P:3 * P], s[:, P:2 * P], s[:, 2 * P:4 * P],
                          start=True, stop=True).then_inc(score_ps, 1)

            def transpose_probs(h):
                pe.wait_ge(probs_ready, h + 1)
                if h >= 2:
                    pe.wait_ge(probsT_ready, h - 1)
                for n in range(3):
                    mm = pe.transpose(psum[:, 4 + h % 2, n * P:(n + 1) * P],
                                      probs[:, h % 2, n * P:(n + 1) * P], ident[:])
                mm.then_inc(probsT_ps, 1)

            def values(h):
                g, r = h // 2, (h % 2) * V
                pe.wait_ge(probsT_ready, h + 1)
                if h % 2 == 0 and g >= 2:
                    pe.wait_ge(o_lo, g - 1)
                p_ = probs_T[:, h % 2]
                pe.matmul(psum[r:r + V, 6 + g % 2, 0:T], v[:, 0, h * V:(h + 1) * V], p_[:, 0:T],
                          start=True, stop=False)
                mm = pe.matmul(psum[r:r + V, 6 + g % 2, P:T], v[:, 1, h * V:(h + 1) * V], p_[:, T:3 * P],
                               start=False, stop=True)
                if h % 2 == 1:
                    mm.then_inc(o_ps, 1)

            pe.wait_ge(qk_ready, TT)
            pe.wait_ge(kv_copied_a, 4 * TT)
            pe.wait_ge(kv_copied_v, 4 * TT)
            transpose_qk(0)
            transpose_qk(1)
            scores(0)
            for h in range(HEADS):
                if h + 1 < HEADS:
                    scores(h + 1)
                transpose_probs(h)
                if h + 2 < HEADS:
                    transpose_qk(h + 2)
                values(h)

            def out_projection(use, first, hT, lT, done):
                for t in range(TT):
                    for b in range(2):
                        terms, marks = [], {}
                        last = t == TT - 1 and b == 1
                        for a in range(KT):
                            s = use(first + a // 2)[0]
                            if t == 0 and b == 0 and a % 2 == 0:
                                ready(pe, use(first + a // 2))
                            tok, cols = slice(t * P, (t + 1) * P), slice(b * BANK, (b + 1) * BANK)
                            terms.append((hT[:, a, tok], lT[:, a, tok], unit(w_hi, s, D)[:, a % 2, cols],
                                          unit(w_lo, s, D)[:, a % 2, cols]))
                            if last and a % 2 == 1:
                                marks[a] = used[s]
                        if not last:
                            marks[KT - 1] = done
                        product(pe, psum[:, 2 * t + b], terms, marks=marks)

            pe.wait_ge(o_lo, HEADS // 2)
            pe.wait_ge(probsT_ready, HEADS)
            out_projection(mla_use, W_O, xTh_mla, xTl_mla, proj_ps)

            transpose_tokens(pe, 1, xn_ffn)
            pe.wait_ge(xT_lo, 8)
            for b in range(4):
                pe.matmul(psum[:, 4 + b, 0:P], zeros[:], zeros[:], start=True, stop=False, skip_group_check=True)
            with pe.Fori(0, STEPS) as i:
                def half_layer(w, t, bank, marks):
                    if t == 0:
                        for s in (2 * w, 2 * w + 1):
                            ready(pe, (s, i + FFN_BASE + 1))
                    tok = slice(t * P, (t + 1) * P)
                    product(pe, psum[:, bank], [
                        (xTh_ffn[:, a, tok], xTl_ffn[:, a, tok], unit(w_hi, 2 * w + a // 4, BANK)[:, a % 4],
                         unit(w_lo, 2 * w + a // 4, BANK)[:, a % 4]) for a in range(KT)], marks=marks)

                def transpose_hidden(t):
                    pe.wait_ge(f_hid, i * TT + (t + 1))
                    for a in range(4):
                        mm = pe.transpose(psum[:, 2 * t, a * P:(a + 1) * P], hid_f[:, t, a * P:(a + 1) * P], ident[:])
                    mm.then_inc(fT_ps, 1)

                def down(t, b, marks):
                    product(pe, psum[:, 4 + 2 * t + b], [
                        (hTh_f[:, t, a], hTl_f[:, t, a],
                         unit(w_hi, 4 + a // 2, D)[:, a % 2, b * BANK:(b + 1) * BANK],
                         unit(w_lo, 4 + a // 2, D)[:, a % 2, b * BANK:(b + 1) * BANK]) for a in range(4)],
                        start=False, stop=False, marks=marks)

                half_layer(0, 0, 0, {KT - 1: fg_ps})
                half_layer(1, 0, 1, {KT - 1: fu_ps})
                half_layer(0, 1, 2, {3: used[0], 7: used[1]})
                transpose_hidden(0)
                half_layer(1, 1, 3, {3: used[2], 7: used[3]})
                for s in (4, 5):
                    ready(pe, (s, i + FFN_BASE + 1))
                pe.wait_ge(fT_lo, i * TT + 1)
                down(0, 0, {})
                transpose_hidden(1)
                down(0, 1, {})
                pe.wait_ge(fT_lo, i * TT + 2)
                down(1, 0, {})
                down(1, 1, {1: used[4], 3: used[5]})

            transpose_tokens(pe, 2, xn_lru)
            pe.wait_ge(xT_lo, 12)

            def channels(first, c, bank, done):
                s, n = lru_use(first + c // 2)
                if c % 2 == 0:
                    ready(pe, (s, n))
                cols = slice((c % 2) * P, (c % 2 + 1) * P)
                product(pe, psum[:, bank, 0:T], [
                    (unit(w_hi, s, 256)[:, a, cols], unit(w_lo, s, 256)[:, a, cols], xTh_lru[:, a], xTl_lru[:, a])
                    for a in range(KT)], marks={KT - 1: done if c % 2 == 0 else used[s]})

            for c in range(KT):
                channels(L_X, c, c, xbr_ps)
            for c in range(KT):
                if c < 4:
                    pe.wait_ge(xbr_copied, 4 + c + 1)
                else:
                    pe.wait_ge(gate_copied, c - 3)
                channels(L_G, c, 4 + c % 4, gate_ps)
                s, n = lru_use(L_AX)
                if c == 0:
                    ready(pe, (s, n))
                pe.wait_ge(xc_lo, c + 1)
                for g in range(2):
                    wg_hi = unit(w_hi, s, P)[:, g * KT + c]
                    wg_lo = unit(w_lo, s, P)[:, g * KT + c]
                    product(pe, psum[:, c % 4, g * T:(g + 1) * T], [(wg_hi, wg_lo, xch[:], xcl[:])],
                            marks={} if g == 0 else {0: ri_ps if c < KT - 1 else used[s]})
            pe.wait_ge(yT_lo, 2)
            pe.wait_ge(ri_exp, 2 * KT)
            out_projection(lru_use, L_OUT, xTh_lru, xTl_lru, out_ps)

            transpose_tokens(pe, 3, xn_moe)
            pe.wait_ge(xT_lo, 16)
            pe.wait_ge(wr_lo_s, 1)
            for t in range(TT):
                tok = slice(t * P, (t + 1) * P)
                product(pe, psum[:, 4 + t, 0:E], [(xTh_moe[:, a, tok], xTl_moe[:, a, tok], wr_hi[:, a], wr_lo[:, a])
                                                  for a in range(KT)], marks={KT - 1: logit_ps})
            pe.wait_ge(mask_ready, 1)
            pe.wait_ge(moe_const, 6)
            sel = rt[:, 6]
            pe.matmul(psum[:, 6, 0:E], before[:], sel[:, 0], start=True, stop=True)
            pe.matmul(psum[:, 6, E:2 * E], before[:], sel[:, 1], start=True, stop=False)
            pe.matmul(psum[:, 6, E:2 * E], ones[:], sel[:, 0], start=False, stop=True)
            pe.matmul(psum[:, 6, 2 * E:3 * E], ones[:], sel[:, 0], start=True, stop=False)
            pe.matmul(psum[:, 6, 2 * E:3 * E], ones[:], sel[:, 1], start=False, stop=True).then_inc(rank_ps, 1)
            pe.wait_ge(plan_ready, 1)
            n_pass = pe.value_load(n_pass_i[0:1, 0:1], min_val=1, max_val=2)

            def gather(n):
                pe.wait_ge(onehot_ready, n * 2)
                for b in range(2):
                    for a in range(4):
                        kt = 4 * b + a
                        for t in range(TT):
                            cols = slice(kt * P, (kt + 1) * P)
                            o = psum[:, 6 + b, a * P:(a + 1) * P]
                            pe.matmul(o, xn_hi[:, t, cols], onehot[:, t], start=t == 0, stop=False)
                            mm = pe.matmul(o, xn_lo[:, t, cols], onehot[:, t], start=False, stop=t == TT - 1)
                    mm.then_inc(gather_ps, 1)

            def transpose_onehot():
                for t in range(TT):
                    mm = pe.transpose(psum[:, 1, 256 + t * P:256 + (t + 1) * P], onehot[:, t].bitcast(F32), ident[:])
                mm.then_inc(ohT_ps, 1)

            def use(s, step):
                return s, step + (MOE_BASE[s] + 1)

            def expert_step(step, first=None, last=None):
                def half_layer(w, f, bank, marks):
                    if f == 0:
                        for s in (2 * w, 2 * w + 1):
                            ready(pe, use(s, step))
                    cols = slice(f * 256, (f + 1) * 256)
                    product(pe, psum[:, bank, 0:256], [
                        (xg_hi[:, a], xg_lo[:, a], unit(w_hi, 2 * w + a // 4, BANK)[:, a % 4, cols],
                         unit(w_lo, 2 * w + a // 4, BANK)[:, a % 4, cols]) for a in range(KT)], marks=marks)

                def transpose_hidden(f):
                    pe.wait_ge(m_hid, step * 2 + (f + 1))
                    for a in range(2):
                        mm = pe.transpose(psum[:, 2 * f, 256 + a * P:256 + (a + 1) * P],
                                          hid_m[:, (2 * f + a) * P:(2 * f + a + 1) * P], ident[:])
                    mm.then_inc(mT_ps, 1)

                def down(f, b, marks):
                    product(pe, psum[:, 4 + b], [
                        (hTh_m[:, 2 * f + a], hTl_m[:, 2 * f + a],
                         unit(w_hi, 4 + f, D)[:, a, b * BANK:(b + 1) * BANK],
                         unit(w_lo, 4 + f, D)[:, a, b * BANK:(b + 1) * BANK]) for a in range(2)],
                        start=False, stop=False, marks=marks)

                half_layer(0, 0, 0, {KT - 1: mg_ps})
                half_layer(1, 0, 1, {KT - 1: mu_ps})
                if first is not None:
                    combine(first, 0)
                half_layer(0, 1, 2, {3: used[0], 7: used[1]})
                if first is not None:
                    combine(first, 1)
                transpose_hidden(0)
                if first is not None:
                    transpose_onehot()
                half_layer(1, 1, 3, {3: used[2], 7: used[3]})
                if first is not None:
                    for b in range(2):
                        pe.matmul(psum[:, 4 + b, 0:P], zeros[:], zeros[:], start=True, stop=False,
                                  skip_group_check=True)
                if last is not None:
                    pe.wait_ge(added, last * 4 + 5)
                    gather(last + 2)
                ready(pe, use(4, step))
                pe.wait_ge(mT_lo, step * 2 + 1)
                down(0, 0, {})
                transpose_hidden(1)
                down(0, 1, {1: used[4]})
                ready(pe, use(5, step))
                pe.wait_ge(mT_lo, step * 2 + 2)
                down(1, 0, {})
                down(1, 1, {1: used[5]})

            def combine(count, t):
                if t == 0:
                    pe.wait_ge(y_lo_s, count * 2 + 2)
                    pe.wait_ge(ohT_ready, count + 1)
                    pe.wait_ge(xg_lo_s, count * 2 + 2)
                else:
                    pe.wait_ge(added, count * 4 + 3)
                for b in range(2):
                    cols = slice(b * BANK, (b + 1) * BANK)
                    pe.matmul(psum[:, 6 + b], onehot_T[:, t], y_hi[:, cols], start=True, stop=False)
                    pe.matmul(psum[:, 6 + b], onehot_T[:, t], y_lo[:, cols], start=False,
                              stop=True).then_inc(comb_ps, 1)

            with pe.Fori(0, n_pass) as p:
                pe.wait_ge(added, p * (4 * (E + 1)) + 1)
                for b in range(2):
                    for a in range(4):
                        pe.matmul(psum[:, 4 + b, a * P:(a + 1) * P], zeros[:], zeros[:], start=True, stop=True)
                gather(p * (E + 1) + 1)
                transpose_onehot()
                with pe.Fori(0, E) as e:
                    count, step = p * (E + 1) + e, p * (E * STEPS) + e * STEPS
                    pe.wait_ge(xg_lo_s, count * 2 + 2)
                    pe.wait_ge(ohT_ready, count + 1)
                    expert_step(step, first=count)
                    with pe.Fori(1, STEPS - 1) as j:
                        expert_step(p * (E * STEPS) + e * STEPS + j)
                    expert_step(step + (STEPS - 1), last=count)
                for t in range(TT):
                    combine(p * (E + 1) + E, t)

        @block.vector
        def _(dve):
            links = [0]
            var_count = [0]

            def link(ins):
                links[0] += 1
                ins.then_inc(link_s, 1)
                dve.wait_ge(link_s, links[0])
                return ins

            def inverse_rms(n, src, scratch, width, at=0):
                for i in range(n):
                    link(dve.tensor_tensor_reduce(scratch[i], src[i], src[i], 1.0, 0.0, ALU.mult, ALU.add,
                                                  sumsq[:, at + i:at + i + 1]))
                s = slice(at, at + n)
                link(dve.tensor_scalar(rstd[:, s], sumsq[:, s], 1.0 / width, RMS_EPS, ALU.mult, ALU.add))
                dve.sem_inc(var_ready, 1)
                var_count[0] += 1
                dve.wait_ge(rstd_ready, var_count[0])

            def norm(phase, xn, gain, arrived, done=xn_ready):
                inverse_rms(TT, [res[:, t] for t in range(TT)], [xn[:, t] for t in range(TT)], D)
                dve.wait_ge(arrived, 16)
                for t in range(TT):
                    dve.scalar_tensor_tensor(out=xn[:, t], in0=res[:, t], scalar=rstd[:, t:t + 1], in1=gain[:],
                                             op0=ALU.mult, op1=ALU.mult).then_inc(done, 1)

            def rope_angles():
                dve.wait_ge(small_in, 16 * 6)
                dve.tensor_copy(pos_f, pos_i).then_inc(cols_ready, 1)
                dve.wait_ge(rows_ps, 2)
                link(dve.tensor_copy(pos_col[:], psum[:, 4, 0:TT]))
                dve.sem_inc(cols_ready, 1)
                dve.tensor_copy(par[:], psum[:, 5, 0:64]).then_inc(cols_ready, 1)
                dve.wait_ge(const, 3 + HALF)
                for t in range(TT):
                    link(dve.tensor_scalar(ang[:, t], inv_freq[:], pos_col[:, t:t + 1], None, ALU.mult))
                two_pi = 2.0 * np.pi
                c1 = 6.28125
                c2 = float(np.floor((two_pi - c1) * 2.0 ** 21) / 2.0 ** 21)
                c3 = float(two_pi - c1 - c2)
                for n, shift in enumerate([0.0, 0.25]):
                    tn = turns[:, n]
                    link(dve.tensor_scalar(tn, ang[:], 1.0 / two_pi, shift, ALU.mult, ALU.add))
                    link(dve.tensor_scalar(tn, tn, ROUND, None, ALU.add))
                    link(dve.tensor_scalar(tn, tn, -ROUND, None, ALU.add))
                    src = ang[:]
                    for c in (c1, c2, c3):
                        link(dve.scalar_tensor_tensor(out=red[:, n], in0=tn, scalar=-c, in1=src,
                                                      op0=ALU.mult, op1=ALU.add))
                        src = red[:, n]
                link(dve.tensor_scalar(red[:, 1], red[:, 1], float(np.pi / 2), None, ALU.add))
                pi = float(np.nextafter(np.float32(np.pi), np.float32(0)))
                dve.tensor_scalar(red[:], red[:], pi, -pi, ALU.min, ALU.max).then_inc(angles, 1)

            for t in range(TT):
                dve.wait_ge(x_in[t], 16)
            norm(0, xn_mla, gain_mla, gain_in[0])
            rope_angles()
            for n in range(W_IN, W_UQ):
                split_lo(dve, mla_use(n), IN_TILES[n][1] * LAT)
            xT_low(dve, 0, xTl_mla, xTh_mla)
            for n in range(W_UQ, W_UKV):
                split_lo(dve, mla_use(n), UQ)
            dve.wait_ge(lat_ready, 2 * TT)
            parts = [(0, QR), (QR, QR + KVR)]
            for n, (c0, c1) in enumerate(parts):
                inverse_rms(TT, [latent[:, t, c0:c1] for t in range(TT)],
                            [v[:, t, c0:c1] for t in range(TT)], c1 - c0, at=n * TT)
            dve.wait_ge(gain_in[1], 16)
            dve.wait_ge(gain_lat, 16)
            for t in range(TT):
                for n, (c0, c1) in enumerate(parts):
                    ins = dve.scalar_tensor_tensor(
                        out=latent[:, t, c0:c1], in0=latent[:, t, c0:c1],
                        scalar=rstd[:, n * TT + t:n * TT + t + 1], in1=gain_mla[:, c0:c1],
                        op0=ALU.mult, op1=ALU.mult)
                    if n == 0:
                        link(ins)
                    else:
                        ins.then_inc(c_ready, 1)
            for n in range(W_UKV, W_O):
                split_lo(dve, mla_use(n), UKV)
            for t in range(TT):
                for b, n in enumerate([4, 1]):
                    dve.wait_ge(c_hi_s, 2 * t + b + 1)
                    area = (slice(None), slice(4 * b, 4 * b + n), slice(t * P, (t + 1) * P))
                    dve.tensor_tensor(c_lo[area], psum[:, 2 * t + b, 0:n * P].rearrange("p (a b) -> p a b", b=P),
                                      c_hi[area].bitcast(F32), ALU.subtract).then_inc(c_lo_s, 1)
            for n in range(W_O, W_O + 2):
                split_lo(dve, mla_use(n))
            for t in range(TT):
                for b in (2, 3):
                    if t == TT - 1 and b == 3:
                        dve.wait_ge(used[mla_use(W_O - 1)[0]], mla_use(W_O - 1)[1])
                    else:
                        dve.wait_ge(kv_ps, 4 * t + b + 1)
                    src = psum[:, KV_BANKS[t][b]].rearrange("p (h c) -> p h c", h=4)
                    dve.tensor_copy(k[:, t, 4 * b:4 * b + 4, 0:NOPE], src[:, :, 0:NOPE]).then_inc(kv_copied_v, 1)
                    dve.tensor_copy(v[:, t, 4 * b * V:4 * (b + 1) * V].rearrange("p (h c) -> p h c", h=4),
                                    src[:, :, NOPE:NOPE + V]).then_inc(kv_copied_v, 1)
            for n in range(W_O + 2, W_O + 4):
                split_lo(dve, mla_use(n))

            def maxima(h):
                b = h % 2
                dve.wait_ge(score_ps, h + 1)
                if h >= 2:
                    dve.wait_ge(probsT_ps, h - 1)
                for r, (c0, c1) in enumerate([(0, P), (P, 3 * P)]):
                    link(dve.tensor_tensor_reduce(probs[:, b, c0:c1], psum[:, 2 + b, c0:c1],
                                                  mask[:, 2 * P - (c1 - c0):2 * P], 1.0,
                                                  -BIG, ALU.add, ALU.max, mx[:, 2 * b + r:2 * b + r + 1]))
                dve.tensor_scalar(nmx[:, 2 * b:2 * b + 2], mx[:, 2 * b:2 * b + 2], -SCALE, None,
                                  ALU.mult).then_inc(max_ready, 1)

            def normalize(h):
                b = h % 2
                dve.wait_ge(exp_ready, 2 * h + 2)
                link(dve.reciprocal(inv[:, 2 * b:2 * b + 2], tot[:, 2 * b:2 * b + 2]))
                link(dve.tensor_scalar(probs[:, b, 0:P], probs[:, b, 0:P], inv[:, 2 * b:2 * b + 1], None, ALU.mult))
                dve.tensor_scalar(probs[:, b, P:3 * P], probs[:, b, P:3 * P], inv[:, 2 * b + 1:2 * b + 2], None,
                                  ALU.mult).then_inc(probs_ready, 1)

            def o_low(g):
                dve.wait_ge(o_hi, g + 1)
                dve.tensor_tensor(xTl_mla[:, g, :], psum[:, 6 + g % 2, 0:T], xTh_mla[:, g, :].bitcast(F32),
                                  ALU.subtract).then_inc(o_lo, 1)

            for h in range(HEADS + 4):
                if h < HEADS:
                    maxima(h)
                if 1 <= h <= HEADS:
                    normalize(h - 1)
                if h >= 4 and h % 2 == 0 and (h - 4) // 2 < HEADS // 2:
                    o_low((h - 4) // 2)
            dve.wait_ge(o_ps, HEADS // 2)
            dve.sem_inc(heads_over, 1)

            def add_projection(done, last_use):
                for t in range(TT):
                    for b in range(2):
                        if t == TT - 1 and b == 1:
                            dve.wait_ge(used[last_use[0]], last_use[1])
                        else:
                            dve.wait_ge(done, 2 * t + b + 1)
                        r = res[:, t, b * BANK:(b + 1) * BANK]
                        link(dve.tensor_tensor(r, r, psum[:, 2 * t + b], ALU.add))

            dve.wait_ge(x_again, 16)
            add_projection(proj_ps, mla_use(W_O + 3))

            norm(1, xn_ffn, gain_ffn, gain_in[2])
            xT_low(dve, 1, xTl_ffn, xTh_ffn)
            with dve.Fori(0, STEPS) as i:
                for s in range(5):
                    split_lo(dve, (s, i + FFN_BASE + 1))
                for t in range(TT):
                    dve.wait_ge(f_tanh, i * TT + (t + 1))
                    dve.scalar_tensor_tensor(out=hid_f[:, t], in0=hid_f[:, t], scalar=1.0, in1=psum[:, 2 * t],
                                             op0=ALU.add, op1=ALU.mult).then_inc(f_mid, 1)
                    dve.wait_ge(f_mid, i * TT + (t + 1))
                    if t == 0:
                        dve.wait_ge(fu_ps, i + 1)
                    else:
                        dve.wait_ge(used[3], i + FFN_BASE + 1)
                    dve.scalar_tensor_tensor(out=hid_f[:, t], in0=hid_f[:, t], scalar=0.5, in1=psum[:, 2 * t + 1],
                                             op0=ALU.mult, op1=ALU.mult).then_inc(f_hid, 1)
                    dve.wait_ge(fT_hi, i * TT + (t + 1))
                    dve.tensor_tensor(hTl_f[:, t], psum[:, 2 * t].rearrange("p (a b) -> p a b", b=P),
                                      hTh_f[:, t].bitcast(F32), ALU.subtract).then_inc(fT_lo, 1)
            dve.wait_ge(used[5], FFN_BASE + STEPS)
            for t in range(TT):
                for b in range(2):
                    r = res[:, t, b * BANK:(b + 1) * BANK]
                    link(dve.tensor_tensor(r, r, psum[:, 4 + 2 * t + b], ALU.add))
            dve.sem_inc(ffn_added, 1)

            norm(2, xn_lru, gain_lru[:, 0:D], gain_in[3])
            for n in range(L_X, L_AX):
                split_lo(dve, lru_use(n))
            xT_low(dve, 2, xTl_lru, xTh_lru)
            CB, BA, LAM = 32, 40, 56
            link(dve.tensor_scalar(neg_b[:], par[:, BA:BA + 2 * KT], -1.0, None, ALU.mult))
            dve.scalar_tensor_tensor(out=sp_t[:, 1], in0=par[:, LAM:LAM + KT], scalar=-1.0,
                                     in1=par[:, LAM:LAM + KT], op0=ALU.mult, op1=ALU.max).then_inc(sp_in, 1)
            link(dve.tensor_scalar(sp_t[:, 2], par[:, LAM:LAM + KT], -1.0, 0.0, ALU.mult, ALU.max))
            dve.wait_ge(sp_exp, 1)
            link(dve.tensor_scalar(sp_t[:, 3], sp_t[:, 0], 2.0, None, ALU.add))
            link(dve.reciprocal(sp_t[:, 3], sp_t[:, 3]))
            link(dve.tensor_tensor(sp_t[:, 3], sp_t[:, 0], sp_t[:, 3], ALU.mult))
            link(dve.tensor_tensor(sp_t[:, 4], sp_t[:, 3], sp_t[:, 3], ALU.mult))
            link(dve.memset(sp_t[:, 5], 0.0))
            for n in range(9, 0, -1):
                link(dve.scalar_tensor_tensor(out=sp_t[:, 5], in0=sp_t[:, 5], scalar=1.0 / (2 * n + 1),
                                              in1=sp_t[:, 4], op0=ALU.add, op1=ALU.mult))
            link(dve.scalar_tensor_tensor(out=sp_t[:, 5], in0=sp_t[:, 5], scalar=1.0, in1=sp_t[:, 3],
                                          op0=ALU.add, op1=ALU.mult))
            link(dve.scalar_tensor_tensor(out=sp_t[:, 6], in0=sp_t[:, 5], scalar=2.0, in1=sp_t[:, 2],
                                          op0=ALU.mult, op1=ALU.add))
            link(dve.tensor_scalar(sp_t[:, 7], sp_t[:, 6], -8.0, None, ALU.mult))
            split_lo(dve, lru_use(L_AX))
            split_lo(dve, lru_use(L_G))

            def conv(c):
                b = c % 2
                dve.wait_ge(xbr_copied, c + 1)
                if c == 0:
                    dve.wait_ge(pads, 1)
                link(dve.tensor_scalar(xc[:, b], x_br[:, c, 0:T], par[:, c:c + 1], par[:, CB + c:CB + c + 1],
                                       ALU.mult, ALU.add))
                for w in range(1, CONV):
                    ins = dve.scalar_tensor_tensor(out=xc[:, b], in0=x_br[:, c, w:w + T],
                                                   scalar=par[:, w * KT + c:w * KT + c + 1], in1=xc[:, b],
                                                   op0=ALU.mult, op1=ALU.add)
                    if w < CONV - 1:
                        link(ins)
                ins.then_inc(xc_ready, 1)

            def xc_low(c):
                dve.wait_ge(xc_hi, c + 1)
                dve.tensor_tensor(xcl[:], xc[:, c % 2], xch[:].bitcast(F32), ALU.subtract).then_inc(xc_lo, 1)

            def squared_multiplier(c):
                dve.wait_ge(a_ready, 2 * (c + 1))
                link(dve.tensor_tensor(a_sq[:], decay[:, c], decay[:, c], ALU.mult))
                dve.scalar_tensor_tensor(out=states[:, c], in0=a_sq[:], scalar=1.0, in1=states[:, c],
                                         op0=ALU.add, op1=ALU.mult).then_inc(mult_in, 1)
                dve.wait_ge(mult_in, c + 1)

            def scans(h):
                s4 = slice(4 * h, 4 * h + 4)
                dve.wait_ge(mult_ready, h + 1)
                link(dve.tensor_tensor(drive[:, s4], drive[:, s4], states[:, s4], ALU.mult))
                for c in range(4 * h, 4 * h + 4):
                    dve.tensor_tensor_scan(states[:, c], decay[:, c], drive[:, c], 0.0, ALU.mult,
                                           ALU.add).then_inc(state_ready, 1)

            conv(0)
            xc_low(0)
            for n in range(1, 4):
                split_lo(dve, lru_use(L_G + n))
            for c in range(KT):
                b = c % 2
                if c + 1 < KT:
                    conv(c + 1)
                for g, dst in enumerate([decay[:, c], drive[:, c]]):
                    dve.wait_ge(ri_exp, 2 * c + g + 1)
                    link(dve.tensor_scalar(dst, dst, 1.0, None, ALU.add))
                    link(dve.reciprocal(dst, dst))
                    if g == 0:
                        dve.tensor_scalar(dst, dst, sp_t[:, 7, c:c + 1], None, ALU.mult).then_inc(log_a, 1)
                link(dve.tensor_tensor(drive[:, c], drive[:, c], xc[:, b], ALU.mult))
                if c + 1 < KT:
                    xc_low(c + 1)
                if c > 0:
                    squared_multiplier(c - 1)
                if c == 6:
                    scans(0)
                if c == 5:
                    split_lo(dve, lru_use(L_OUT))
                if c == 6:
                    split_lo(dve, lru_use(L_OUT + 2))
            squared_multiplier(KT - 1)
            scans(1)
            dve.wait_ge(state_ready, KT)
            dve.wait_ge(gelu_ready, 1)
            for h in range(2):
                s4 = slice(4 * h, 4 * h + 4)
                dve.tensor_tensor(states[:, s4], states[:, s4], gate_br[:, s4], ALU.mult).then_inc(y_ready, 1)
            split_lo(dve, lru_use(L_OUT + 1))
            for h in range(2):
                s4 = slice(4 * h, 4 * h + 4)
                dve.wait_ge(yT_hi, h + 1)
                dve.tensor_tensor(xTl_lru[:, s4], states[:, s4], xTh_lru[:, s4].bitcast(F32),
                                  ALU.subtract).then_inc(yT_lo, 1)
            split_lo(dve, lru_use(L_OUT + 3))
            add_projection(out_ps, lru_use(L_OUT + 3))
            dve.sem_inc(lru_added, 1)

            norm(3, xn_moe, gain_moe, gain_in[4])
            xT_low(dve, 3, xTl_moe, xTh_moe)
            dve.wait_ge(wr_hi_s, 1)
            dve.tensor_tensor(wr_lo[:], wr[:], wr_hi[:].bitcast(F32), ALU.subtract).then_inc(wr_lo_s, 1)
            dve.wait_ge(logit_ps, TT)
            lg = rt[:, 0]
            link(dve.tensor_copy(lg, psum[:, 4:4 + TT, 0:E]))
            dve.wait_ge(xnh_ready, TT)
            for t in range(TT):
                link(dve.tensor_tensor(xn_lo[:, t], xn_moe[:, t], xn_hi[:, t].bitcast(F32), ALU.subtract))
            dve.wait_ge(moe_const, 6)

            def spread(a):
                return a.unsqueeze(2).broadcast_to([P, TT, E])

            def first_of_max(src, top, tmp, hot):
                link(dve.tensor_reduce(top, src, AX, ALU.max))
                link(dve.tensor_tensor(tmp, src, spread(top), ALU.is_equal))
                link(dve.scalar_tensor_tensor(out=tmp, in0=tmp, scalar=-64.0, in1=expert_no[:], op0=ALU.mult,
                                              op1=ALU.add))
                link(dve.tensor_reduce(rs[:, 7], tmp, AX, ALU.min))
                link(dve.tensor_tensor(hot, tmp, spread(rs[:, 7]), ALU.is_equal))

            first_of_max(lg, rs[:, 0], rt[:, 1], rt[:, 2])
            link(dve.scalar_tensor_tensor(out=rt[:, 3], in0=rt[:, 2], scalar=-BIG, in1=lg, op0=ALU.mult,
                                          op1=ALU.add))
            first_of_max(rt[:, 3], rs[:, 1], rt[:, 1], rt[:, 4])
            dve.tensor_tensor(rs[:, 2], rs[:, 1], rs[:, 0], ALU.subtract).then_inc(top_diff, 1)
            dve.tensor_tensor(rt[:, 6], rt[:, 2], rt[:, 4], ALU.add).then_inc(mask_ready, 1)
            dve.wait_ge(top_exp, 1)
            link(dve.tensor_scalar(rs[:, 4], rs[:, 3], 1.0, None, ALU.add))
            link(dve.reciprocal(rs[:, 4], rs[:, 4]))
            link(dve.tensor_tensor(rs[:, 5], rs[:, 3], rs[:, 4], ALU.mult))
            link(dve.tensor_tensor(rt[:, 5], rt[:, 2], spread(rs[:, 4]), ALU.mult))
            link(dve.tensor_tensor(rt[:, 7], rt[:, 4], spread(rs[:, 5]), ALU.mult))
            link(dve.memset(gates[:, :, 0:1], 0.0))
            link(dve.tensor_tensor(gates[:, :, 1:E + 1], rt[:, 5], rt[:, 7], ALU.add))
            dve.wait_ge(rank_ps, 1)
            ranks = psum[:, 6, 0:2 * E].rearrange("p (t e) -> p t e", e=E)
            link(dve.scalar_tensor_tensor(out=rt[:, 1], in0=ranks, scalar=1.0, in1=rt[:, 6], op0=ALU.add,
                                          op1=ALU.mult))
            link(dve.tensor_scalar(key[:, :, 0:E], rt[:, 1], -1.0, None, ALU.add))
            link(dve.tensor_reduce(rs[:, 6, 0:1], psum[:, 6, 2 * E:3 * E], AX, ALU.max))
            dve.tensor_scalar(n_pass_i[:], rs[0:1, 6, 0:1], float(SLOT_TOKENS), 1.0, ALU.is_gt,
                              ALU.add).then_inc(plan_ready, 1)
            dve.sem_inc(added, 1)
            dve.wait_ge(plan_ready, 1)
            n_pass = dve.value_load(n_pass_i[0:1, 0:1], min_val=1, max_val=2)

            def one_hot(e):
                for t in range(TT):
                    dve.tensor_scalar(onehot[:, t], slot_no[:], key[:, t, bass.ds(e, 1)], None,
                                      ALU.is_equal).then_inc(onehot_ready, 1)

            def xg_low(n):
                for b in range(2):
                    dve.wait_ge(xg_hi_s, n * 2 + (b - 1))
                    dve.tensor_tensor(xg_lo[:, 4 * b:4 * b + 4, :], psum[:, 6 + b].rearrange("p (a b) -> p a b", b=P),
                                      xg_hi[:, 4 * b:4 * b + 4, :].bitcast(F32), ALU.subtract).then_inc(xg_lo_s, 1)

            def use(s, step):
                return s, step + (MOE_BASE[s] + 1)

            def y_low(n):
                for b in range(2):
                    cols = slice(b * BANK, (b + 1) * BANK)
                    dve.wait_ge(y_hi_s, n * 2 + (b - 1))
                    dve.tensor_tensor(y_lo[:, cols], psum[:, 4 + b], y_hi[:, cols].bitcast(F32),
                                      ALU.subtract).then_inc(y_lo_s, 1)

            def add_results(count, e, t):
                for b in range(2):
                    dve.wait_ge(comb_ps, count * 4 + (2 * t + b + 1))
                    r = res[:, t, b * BANK:(b + 1) * BANK]
                    dve.scalar_tensor_tensor(out=r, in0=psum[:, 6 + b], scalar=gates[:, t, bass.ds(e, 1)],
                                             in1=r, op0=ALU.mult, op1=ALU.add).then_inc(added, 1)

            def step_work(step, more=True, first=None, last=None):
                def silu(f):
                    cols = slice(256 * f, 256 * (f + 1))
                    dve.wait_ge(m_tanh, step * 2 + (f + 1))
                    dve.scalar_tensor_tensor(out=hid_m[:, cols], in0=hid_m[:, cols], scalar=1.0,
                                             in1=psum[:, 2 * f, 0:256], op0=ALU.add, op1=ALU.mult).then_inc(m_mid, 1)

                def times_up(f):
                    cols = slice(256 * f, 256 * (f + 1))
                    dve.wait_ge(m_mid, step * 2 + (f + 1))
                    if f == 0:
                        dve.wait_ge(mu_ps, step + 1)
                    else:
                        dve.wait_ge(used[3], use(3, step)[1])
                    dve.scalar_tensor_tensor(out=hid_m[:, cols], in0=hid_m[:, cols], scalar=0.5,
                                             in1=psum[:, 2 * f + 1, 0:256], op0=ALU.mult,
                                             op1=ALU.mult).then_inc(m_hid, 1)

                def hT_low(f):
                    dve.wait_ge(mT_hi, step * 2 + (f + 1))
                    dve.tensor_tensor(hTl_m[:, 2 * f:2 * f + 2], psum[:, 2 * f, 256:512].rearrange("p (a b) -> p a b", b=P),
                                      hTh_m[:, 2 * f:2 * f + 2].bitcast(F32), ALU.subtract).then_inc(mT_lo, 1)

                if first is not None:
                    y_low(first[0] + 1)
                split_lo(dve, use(4, step))
                silu(0)
                times_up(0)
                if first is not None:
                    dve.wait_ge(added, first[0] * 4 + 1)
                    add_results(*first, 0)
                silu(1)
                hT_low(0)
                if first is not None:
                    add_results(*first, 1)
                times_up(1)
                if more:
                    split_lo(dve, use(0, step + 1))
                hT_low(1)
                if first is not None:
                    dve.wait_ge(ohT_ps, first[0] + 2)
                    one_hot(first[1] + 1)
                if last is not None:
                    xg_low(last[0] + 2)
                if more:
                    for s in (2, 3):
                        split_lo(dve, use(s, step + 1))

            def expert_work(p, e, more):
                step, count = p * (E * STEPS) + e * STEPS, p * (E + 1) + e
                step_work(step, first=(count, e))
                with dve.Fori(1, STEPS - 1) as j:
                    step_work(step + j)
                step_work(step + (STEPS - 1), more=more, last=(count, e))

            with dve.Fori(0, n_pass) as p:
                one_hot(0)
                xg_low(p * (E + 1) + 1)
                for s in (0, 2, 3):
                    split_lo(dve, use(s, p * (E * STEPS)))
                with dve.Fori(0, E - 1) as e:
                    expert_work(p, e, True)
                expert_work(p, E - 1, False)
                y_low(p * (E + 1) + (E + 1))
                dve.wait_ge(added, p * (4 * (E + 1)) + 4 * E + 1)
                for t in range(TT):
                    add_results(p * (E + 1) + E, E, t)
                dve.tensor_scalar(key[:, :, 0:E], key[:, :, 0:E], float(-SLOT_TOKENS), None,
                                  ALU.add).then_inc(pass_over, 1)
                dve.wait_ge(pass_over, p + 1)
                dve.wait_ge(added, p * (4 * (E + 1)) + 4 * (E + 1) + 1)
            dve.sem_inc(moe_over, 1)
            norm(4, xn_out, gain_out, gain_in[5], out_ready)


_INS = ["x", "positions", "norm_mix", "norm_ffn", "norm_final", "mla_w_in", "mla_q_norm", "mla_kv_norm",
        "mla_w_uq", "mla_w_ukv", "mla_w_o", "lru_w_in", "lru_conv_w", "lru_conv_b", "lru_w_a", "lru_b_a",
        "lru_w_x", "lru_b_x", "lru_lam", "lru_w_out", "ffn_w_gate", "ffn_w_up", "ffn_w_down", "moe_w_router",
        "moe_w_gate", "moe_w_up", "moe_w_down"]


def kernel(**inputs):
    import numpy as _np
    import concourse.bacc as _bacc
    from concourse import mybir as _mybir
    from concourse.bass_utils import run_bass_kernel_spmd as _run

    nc = _bacc.Bacc("TRN2", target_bir_lowering=False, num_devices=1)
    arrays, args = {}, []
    for name in _INS:
        a = _np.ascontiguousarray(inputs[name])
        arrays[f"in_{name}"] = a
        args.append(nc.dram_tensor(f"in_{name}", a.shape, _mybir.dt.from_np(a.dtype), kind="ExternalInput").ap())
    out = nc.dram_tensor("out", inputs["x"].shape, _mybir.dt.float32, kind="ExternalOutput").ap()
    trunk(nc, *args, out)
    r = _run(nc, [arrays], core_ids=[0])
    return r.results[0]["out"]
```

```python
from contextlib import ExitStack

import numpy as np
import concourse.bass as bass
from concourse import mybir

F32 = mybir.dt.float32
F32R = mybir.dt.float32r
BF16 = mybir.dt.bfloat16
I32 = mybir.dt.int32
ALU = mybir.AluOpType
ACT = mybir.ActivationFunctionType
AX = mybir.AxisListType.X

P = 128
BANK = 512
BIG = 3.0e38
ROUND = 1.5 * 2.0 ** 23
RMS_EPS = 1e-6


def trunk(nc, x, positions, norm_mix, norm_ffn, norm_final, mla_w_in, mla_q_norm, mla_kv_norm,
          mla_w_uq, mla_w_ukv, mla_w_o, lru_w_in, lru_conv_w, lru_conv_b, lru_w_a, lru_b_a,
          lru_w_x, lru_b_x, lru_lam, lru_w_out, ffn_w_gate, ffn_w_up, ffn_w_down, moe_w_router,
          moe_w_gate, moe_w_up, moe_w_down, out):
    T, D = x.shape[1], x.shape[2]
    TT, KT = T // P, D // P
    QR, KVR = mla_q_norm.shape[1], mla_kv_norm.shape[1]
    LAT = mla_w_in.shape[2]
    ROPE = LAT - QR - KVR
    HALF = ROPE // 2
    HEADS, V = 16, 64
    NOPE = V
    QK = NOPE + ROPE
    SCALE = float(QK) ** -0.5
    F = ffn_w_gate.shape[2]
    E = moe_w_router.shape[2]
    STEPS = F // BANK
    SLOT_TOKENS = P
    SLOTS = 6
    UNIT = 2048
    CONV = lru_conv_w.shape[1]
    assert T == 256 and D == 1024 and F % BANK == 0 and LAT == 672

    with ExitStack() as ctx:
        def sb(stack, name, shape, dt):
            return stack.enter_context(nc.sbuf_tensor(name, shape, dt))

        def sem(name):
            return ctx.enter_context(nc.semaphore(name))

        raw = sb(ctx, "raw", [P, SLOTS, UNIT], F32)
        w_hi = sb(ctx, "w_hi", [P, SLOTS, UNIT], F32R)
        w_lo = sb(ctx, "w_lo", [P, SLOTS, UNIT], F32R)
        res = sb(ctx, "res", [P, TT, D], F32)
        ident = sb(ctx, "ident", [P, P], F32)
        pos_col = sb(ctx, "pos_col", [P, TT], F32)
        par = sb(ctx, "par", [P, 64], F32)
        inv_freq = sb(ctx, "inv_freq", [P, HALF], F32)
        ang = sb(ctx, "ang", [P, TT, HALF], F32)
        trig = sb(ctx, "trig", [P, 2, TT, HALF], F32)
        sumsq = sb(ctx, "sumsq", [P, 4], F32)
        rstd = sb(ctx, "rstd", [P, 4], F32)
        half = sb(ctx, "half", [P, 1], F32)
        zeros = sb(ctx, "zeros", [P, P], BF16)
        n_pass_i = sb(ctx, "n_pass_i", [1, 1], I32)
        psum = ctx.enter_context(nc.psum_tensor("psum", [P, 8, BANK], F32))

        with ExitStack() as s:
            gain_mla = sb(s, "gain_mla", [P, D], F32)
            xn_mla = sb(s, "xn_mla", [P, TT, D], F32)
            xTh_mla = sb(s, "xTh_mla", [P, KT, T], F32R)
            xTl_mla = sb(s, "xTl_mla", [P, KT, T], F32R)
            q = sb(s, "q", [P, TT, HEADS, QK], F32)
            k = sb(s, "k", [P, TT, HEADS, QK], F32)
            mask = sb(s, "mask", [P, 2 * P], F32)
        with ExitStack() as s:
            gain_ffn = sb(s, "gain_ffn", [P, D], F32)
            xn_ffn = sb(s, "xn_ffn", [P, TT, D], F32)
            xTh_ffn = sb(s, "xTh_ffn", [P, KT, T], F32R)
            xTl_ffn = sb(s, "xTl_ffn", [P, KT, T], F32R)
            hid_f = sb(s, "hid_f", [P, TT, BANK], F32)
            hTh_f = sb(s, "hTh_f", [P, TT, 4, P], F32R)
            hTl_f = sb(s, "hTl_f", [P, TT, 4, P], F32R)
        with ExitStack() as s:
            gain_lru = sb(s, "gain_lru", [P, 2 * D], F32)
            xn_lru = sb(s, "xn_lru", [P, TT, D], F32)
            xTh_lru = sb(s, "xTh_lru", [P, KT, T], F32R)
            xTl_lru = sb(s, "xTl_lru", [P, KT, T], F32R)
            gate_br = sb(s, "gate_br", [P, KT, T], F32)
            x_br = sb(s, "x_br", [P, KT, CONV - 1 + T], F32)
            xch = sb(s, "xch", [P, 2, T], F32R)
            xcl = sb(s, "xcl", [P, 2, T], F32R)
            a_sq = sb(s, "a_sq", [P, T], F32)
            sp_t = sb(s, "sp_t", [P, 8, KT], F32)
        with ExitStack() as s:
            xTh_moe = sb(s, "xTh_moe", [P, KT, T], F32R)
            xTl_moe = sb(s, "xTl_moe", [P, KT, T], F32R)
            xn_hi = sb(s, "xn_hi", [P, TT, D], F32R)
            hid_m = sb(s, "hid_m", [P, BANK], F32)
            hTh_m = sb(s, "hTh_m", [P, 4, P], F32R)
            hTl_m = sb(s, "hTl_m", [P, 4, P], F32R)
            onehot = sb(s, "onehot", [P, TT, SLOT_TOKENS], F32R)
            onehot_T = sb(s, "onehot_T", [P, TT, P], F32R)
            before = sb(s, "before", [P, P], F32)
            ones = sb(s, "ones", [P, P], F32)
            slot_no = sb(s, "slot_no", [P, SLOT_TOKENS], F32)
            expert_no = sb(s, "expert_no", [P, TT, E], F32)
            wr = sb(s, "wr", [P, KT, E], F32)
            wr_hi = sb(s, "wr_hi", [P, KT, E], F32R)
            wr_lo = sb(s, "wr_lo", [P, KT, E], F32R)
            rt = sb(s, "rt", [P, 8, TT, E], F32)
            rs = sb(s, "rs", [P, 8, TT], F32)
            logits_T = sb(s, "logits_T", [E, T], F32)
            key = sb(s, "key", [P, TT, E + 1], F32)
            gates = sb(s, "gates", [P, TT, E + 1], F32)
            gain_out = sb(s, "gain_out", [P, D], F32)
            with ExitStack() as s2:
                gain_moe = sb(s2, "gain_moe", [P, D], F32)
                xn_moe = sb(s2, "xn_moe", [P, TT, D], F32)
            with ExitStack() as s2:
                y_hi = sb(s2, "y_hi", [P, D], F32R)
                y_lo = sb(s2, "y_lo", [P, D], F32R)
            with ExitStack() as s2:
                xn_out = sb(s2, "xn_out", [P, TT, D], F32)

        latent = res[:, :, 0:LAT]
        c_hi, c_lo = xTh_mla, xTl_mla
        rows = k[:, 0].rearrange("p h c -> p (h c)")[:, 0:P]
        angle_area = q[:, 1].rearrange("p h c -> p (h c)")
        pos_area = q[0:TT, 0].rearrange("p h c -> p (h c)")
        pos_f, pos_i = pos_area[:, 0:P], pos_area[:, P:2 * P].bitcast(I32)
        turns = angle_area[:, 0:2 * TT * HALF].rearrange("p (n t c) -> p n t c", n=2, t=TT)
        red = angle_area[:, P:P + 2 * TT * HALF].rearrange("p (n t c) -> p n t c", n=2, t=TT)
        rope_area = res[:, 1, LAT:LAT + HEADS * HALF].rearrange("p (h c) -> p h c", c=HALF)
        qkT = gain_mla.rearrange("p (b n) -> p b n", b=2)
        v = xn_mla
        probs = res[:, 0, 0:6 * P].rearrange("p (b n) -> p b n", b=2)
        probs_T = res[:, 1, 0:6 * P].rearrange("p (b n) -> p b n", b=2)
        att = res[:, 0, 6 * P:8 * P].rearrange("p (a b) -> p a b", b=32)
        mx, nmx, tot, inv = att[:, 0], att[:, 1], att[:, 2], att[:, 3]
        Q_BANKS = [(4, 5, 6), (0, 1, 2)]
        KV_BANKS = [(3, 7, 4, 5), (6, 0, 1, 2)]
        decay = gain_lru.rearrange("p (c t) -> p c t", t=T)
        drive = x_br[:, :, CONV - 1:]
        CB, BA, LAM = 32, 40, 56
        states = xn_lru.rearrange("p a (c t) -> p (a c) t", t=T)
        xg_hi = xTh_moe[:, 0:4, :].rearrange("p a t -> p (a t)").rearrange("p (k t) -> p k t", t=P)
        xg_lo = xTh_moe[:, 4:8, :].rearrange("p a t -> p (a t)").rearrange("p (k t) -> p k t", t=P)
        xn_lo = xTl_moe.rearrange("p k t -> p (k t)").rearrange("p (a d) -> p a d", a=TT)

        landed = [sem(f"landed{n}") for n in range(SLOTS)]
        hi_done = [sem(f"hi_done{n}") for n in range(SLOTS)]
        lo_done = [sem(f"lo_done{n}") for n in range(SLOTS)]
        used = [sem(f"used{n}") for n in range(SLOTS)]
        FFN_BASE = 2
        LRU_BASE = FFN_BASE + STEPS
        MOE_BASE = [LRU_BASE + (13 - s + SLOTS - 1) // SLOTS for s in range(SLOTS)]

        def mla_use(n):
            return n % SLOTS, n // SLOTS + 1

        def lru_use(n):
            return n % SLOTS, LRU_BASE + n // SLOTS + 1

        x_in = [sem(f"x_in{t}") for t in range(TT)]
        x_again = sem("x_again")
        gain_lat = sem("gain_lat")
        wx_landed = sem("wx_landed")
        pass_over = sem("pass_over")
        var_ready = sem("var_ready")
        rstd_ready = sem("rstd_ready")
        mult_in = sem("mult_in")
        mult_ready = sem("mult_ready")
        small_in = sem("small_in")
        gain_in = [sem(f"gain_in{n}") for n in range(6)]
        const = sem("const")
        moe_const = sem("moe_const")
        link_s = sem("link_s")
        xn_ready = sem("xn_ready")
        xT_ps = sem("xT_ps")
        xT_hi = sem("xT_hi")
        xT_lo = sem("xT_lo")
        rows_ps = sem("rows_ps")
        cols_ready = sem("cols_ready")
        angles = sem("angles")
        trig_ready = sem("trig_ready")
        lat_ps = sem("lat_ps")
        lat_ready = sem("lat_ready")
        c_ready = sem("c_ready")
        c_ps = sem("c_ps")
        c_hi_s = sem("c_hi_s")
        c_lo_s = sem("c_lo_s")
        q_ps = sem("q_ps")
        q_copied = sem("q_copied")
        kv_ps = sem("kv_ps")
        kv_copied_a = sem("kv_copied_a")
        kv_copied_v = sem("kv_copied_v")
        pool_link = sem("pool_link")
        qk_ready = sem("qk_ready")
        qkT_ps = sem("qkT_ps")
        qkT_ready = sem("qkT_ready")
        score_ps = sem("score_ps")
        max_ready = sem("max_ready")
        exp_ready = sem("exp_ready")
        probs_ready = sem("probs_ready")
        probsT_ps = sem("probsT_ps")
        probsT_ready = sem("probsT_ready")
        o_ps = sem("o_ps")
        o_hi = sem("o_hi")
        o_lo = sem("o_lo")
        heads_over = sem("heads_over")
        proj_ps = sem("proj_ps")
        fg_ps = sem("fg_ps")
        fu_ps = sem("fu_ps")
        fd_ps = sem("fd_ps")
        f_tanh = sem("f_tanh")
        f_mid = sem("f_mid")
        f_hid = sem("f_hid")
        fT_ps = sem("fT_ps")
        fT_hi = sem("fT_hi")
        fT_lo = sem("fT_lo")
        pads = sem("pads")
        sp_exp = sem("sp_exp")
        sp_in = sem("sp_in")
        xbr_ps = sem("xbr_ps")
        xbr_copied = sem("xbr_copied")
        gate_ps = sem("gate_ps")
        gate_copied = sem("gate_copied")
        xc_ready = sem("xc_ready")
        xc_hi = sem("xc_hi")
        xc_lo = sem("xc_lo")
        ri_ps = sem("ri_ps")
        ri_ready = sem("ri_ready")
        log_a = sem("log_a")
        a_ready = sem("a_ready")
        state_ready = sem("state_ready")
        gelu_ready = sem("gelu_ready")
        y_ready = sem("y_ready")
        yT_hi = sem("yT_hi")
        yT_lo = sem("yT_lo")
        out_ps = sem("out_ps")
        xnh_ready = sem("xnh_ready")
        wr_in = sem("wr_in")
        wr_hi_s = sem("wr_hi_s")
        wr_lo_s = sem("wr_lo_s")
        logit_ps = sem("logit_ps")
        logit_copied = sem("logit_copied")
        xn_lo_ready = sem("xn_lo_ready")
        top_diff = sem("top_diff")
        top_exp = sem("top_exp")
        mask_ready = sem("mask_ready")
        rank_ps = sem("rank_ps")
        plan_ready = sem("plan_ready")
        onehot_ready = sem("onehot_ready")
        gather_ps = sem("gather_ps")
        xg_hi_s = sem("xg_hi_s")
        xg_lo_s = sem("xg_lo_s")
        ohT_ps = sem("ohT_ps")
        ohT_ready = sem("ohT_ready")
        mg_ps = sem("mg_ps")
        mu_ps = sem("mu_ps")
        m_tanh = sem("m_tanh")
        m_mid = sem("m_mid")
        m_hid = sem("m_hid")
        mT_ps = sem("mT_ps")
        mT_hi = sem("mT_hi")
        mT_lo = sem("mT_lo")
        y_hi_s = sem("y_hi_s")
        y_lo_s = sem("y_lo_s")
        comb_ps = sem("comb_ps")
        added = sem("added")
        out_ready = sem("out_ready")
        stored = sem("stored")

        def slab(w, c0, n):
            return w[:, c0:c0 + n].rearrange("(k p) f -> p k f", p=P)

        def row_tiles(w, k0, n):
            return w[k0 * P:(k0 + n) * P, :].rearrange("(k p) f -> p k f", p=P)

        W_IN, W_UQ, W_UKV, W_O = 0, 3, 6, 8
        UQ, UKV = mla_w_uq.shape[2], mla_w_ukv.shape[2]
        IN_TILES = [(0, 3), (3, 3), (6, 2)]
        mla_units = [row_tiles(mla_w_in[0], a, n) for a, n in IN_TILES]
        mla_units += [row_tiles(mla_w_uq[0], a, 1) for a in range(QR // P)]
        mla_units += [row_tiles(mla_w_ukv[0], a, 1) for a in range(KVR // P)]
        mla_units += [row_tiles(mla_w_o[0], 2 * a, 2) for a in range(4)]
        L_X, L_AX, L_G, L_OUT = 0, 4, 5, 9
        lru_units = [slab(lru_w_in[0], D + 256 * u, 256) for u in range(4)]
        lru_units += [None]
        lru_units += [slab(lru_w_in[0], 256 * u, 256) for u in range(4)]
        lru_units += [row_tiles(lru_w_out[0], 2 * a, 2) for a in range(4)]
        ffn_v = [ffn_w_gate.rearrange("e (h k p) (j f) -> e h j p k f", h=2, p=P, f=BANK),
                 ffn_w_up.rearrange("e (h k p) (j f) -> e h j p k f", h=2, p=P, f=BANK),
                 ffn_w_down.rearrange("e (j h r p) d -> e h j p r d", h=2, r=2, p=P)]
        moe_v = [moe_w_gate[0].rearrange("e (h k p) (j f) -> e h j p k f", h=2, p=P, f=BANK),
                 moe_w_up[0].rearrange("e (h k p) (j f) -> e h j p k f", h=2, p=P, f=BANK),
                 moe_w_down[0].rearrange("e (j h r p) d -> e h j p r d", h=2, r=2, p=P)]

        def unit(t, s, b):
            return t[:, s, 0:UNIT // b * b].rearrange("p (a b) -> p a b", b=b)

        def load(sp, use, src):
            s, n = use
            if not isinstance(n, int) or n > 1:
                sp.wait_ge(lo_done[s], n - 1)
            a, b = src.shape[1], src.shape[2]
            dst = raw[:, s, 0:a * b].rearrange("p (a b) -> p a b", b=b)
            sp.dma_start(dst, src).then_inc(landed[s], 16)

        def split_hi(act, use, width=UNIT):
            s, n = use
            act.wait_ge(landed[s], n * 16)
            if not isinstance(n, int) or n > 1:
                act.wait_ge(used[s], n - 1)
            act.activation(w_hi[:, s, 0:width], raw[:, s, 0:width], ACT.Copy).then_inc(hi_done[s], 1)

        def split_lo(eng, use, width=UNIT):
            s, n = use
            eng.wait_ge(hi_done[s], n)
            eng.tensor_tensor(w_lo[:, s, 0:width], raw[:, s, 0:width], w_hi[:, s, 0:width].bitcast(F32),
                              ALU.subtract).then_inc(lo_done[s], 1)

        def ready(pe, use):
            s, n = use
            pe.wait_ge(lo_done[s], n)

        def product(pe, out_ap, terms, start=True, stop=True, marks=(), units=()):
            marks, units = dict(marks), dict(units)
            for n, (sh, sl, mh, ml) in enumerate(terms):
                if n in units:
                    ready(pe, units[n])
                first, last = start and n == 0, stop and n == len(terms) - 1
                lone = dict(skip_group_check=True) if not (start and stop) else {}
                pe.matmul(out_ap, sh, mh, start=first, stop=False, **lone)
                pe.matmul(out_ap, sh, ml, start=False, stop=False, **lone)
                mm = pe.matmul(out_ap, sl, mh, start=False, stop=last, **lone)
                if n in marks:
                    mm.then_inc(marks[n], 1)

        def transpose_tokens(pe, phase, src):
            for t in range(TT):
                pe.wait_ge(xn_ready, TT * phase + t + 1)
                for h in range(2):
                    for a in range(4):
                        kt = 4 * h + a
                        mm = pe.transpose(psum[:, 2 * t + h, a * P:(a + 1) * P],
                                          src[:, t, kt * P:(kt + 1) * P], ident[:])
                    mm.then_inc(xT_ps, 1)

        def xT_high(act, phase, dst):
            for t in range(TT):
                for h in range(2):
                    act.wait_ge(xT_ps, 4 * phase + 2 * t + h + 1)
                    act.activation(dst[:, 4 * h:4 * h + 4, t * P:(t + 1) * P],
                                   psum[:, 2 * t + h].rearrange("p (a b) -> p a b", b=P),
                                   ACT.Copy).then_inc(xT_hi, 1)

        def xT_low(dve, phase, dst, high):
            for t in range(TT):
                for h in range(2):
                    dve.wait_ge(xT_hi, 4 * phase + 2 * t + h + 1)
                    area = (slice(None), slice(4 * h, 4 * h + 4), slice(t * P, (t + 1) * P))
                    dve.tensor_tensor(dst[area], psum[:, 2 * t + h].rearrange("p (a b) -> p a b", b=P),
                                      high[area].bitcast(F32), ALU.subtract).then_inc(xT_lo, 1)

        block = ctx.enter_context(nc.Block())

        @block.sync
        def _(sp):
            for t in range(TT):
                sp.dma_start(res[:, t, :], x[0, t * P:(t + 1) * P, :]).then_inc(x_in[t], 16)
            for n in range(len(mla_units)):
                load(sp, mla_use(n), mla_units[n])
            for s in range(SLOTS):
                load(sp, (s, FFN_BASE + 1), ffn_v[s // 2][0, s % 2, 0])
            sp.wait_ge(heads_over, 1)
            sp.dma_start(res[:], x[0].rearrange("(t p) d -> p t d", p=P)).then_inc(x_again, 16)
            with sp.Fori(1, STEPS) as i:
                for s in range(SLOTS):
                    load(sp, (s, i + FFN_BASE + 1), ffn_v[s // 2][0, s % 2, i])
            for n in range(len(lru_units)):
                s, c = lru_use(n)
                if n != L_AX:
                    load(sp, (s, c), lru_units[n])
                    continue
                sp.wait_ge(lo_done[s], c - 1)
                half = UNIT // 2
                sp.dma_start(raw[:, s, 0:half].rearrange("p (h j) -> p h j", j=P),
                             lru_w_a[0].rearrange("h i j -> i h j")).then_inc(landed[s], 16)
                sp.dma_start(raw[:, s, half:UNIT].rearrange("p (h j) -> p h j", j=P),
                             lru_w_x[0].rearrange("h i j -> i h j")).then_inc(wx_landed, 16)

            def moe_loads(e, j, step):
                for s in range(SLOTS):
                    load(sp, (s, step + (MOE_BASE[s] + 1)), moe_v[s // 2][e, s % 2, j])

            with sp.Fori(0, E) as e:
                with sp.Fori(0, STEPS) as j:
                    moe_loads(e, j, e * STEPS + j)
            sp.wait_ge(plan_ready, 1)
            n_pass = sp.value_load(n_pass_i[0:1, 0:1], min_val=1, max_val=2)
            with sp.If(n_pass > 1):
                with sp.Fori(0, E) as e:
                    with sp.Fori(0, STEPS) as j:
                        moe_loads(e, j, e * STEPS + j + E * STEPS)
            for t in range(TT):
                sp.wait_ge(out_ready, t + 1)
                sp.dma_start(out[0, t * P:(t + 1) * P, :], xn_out[:, t, :]).then_inc(stored, 16)
            sp.wait_ge(stored, 16 * TT)

        @block.gpsimd
        def _(pool):
            links = [0]

            def link(ins):
                links[0] += 1
                ins.then_inc(pool_link, 1)
                pool.wait_ge(pool_link, links[0])

            def gain(n, dst, src):
                pool.dma_start(dst, src.partition_broadcast(P)).then_inc(gain_in[n], 16)

            gain(0, gain_mla[:], norm_mix[0])
            for n, w in enumerate([lru_conv_w[0].rearrange("w (c p) -> (w c) p", p=P)]
                                  + [a[0].rearrange("(c p) -> c p", p=P)
                                     for a in (lru_conv_b, lru_b_a, lru_b_x, lru_lam)]):
                at = 0 if n == 0 else 24 + 8 * n
                pool.dma_start(rows[at:at + w.shape[0], :], w).then_inc(small_in, 16)
            pool.dma_start(pos_i, positions[0].rearrange("(t p) -> t p", p=P)).then_inc(small_in, 16)
            link(pool.memset(ident[:], 0.0))
            link(pool.memset(mask[:], 0.0))
            pool.affine_select(out=ident[:], in_=ident[:], compare_op=ALU.not_equal, fill=1.0, base=0,
                               pattern=[[-1, P]], channel_multiplier=1).then_inc(const, 1)
            pool.affine_select(out=mask[:, P:2 * P], in_=mask[:, P:2 * P], compare_op=ALU.is_ge,
                               fill=-BIG, base=0, pattern=[[-1, P]], channel_multiplier=1).then_inc(const, 1)
            pool.memset(zeros[:], 0.0).then_inc(const, 1)
            link(pool.memset(half[:], -0.5))

            roots = [0]

            def inverse_roots(at, width):
                roots[0] += 1
                pool.wait_ge(var_ready, roots[0])
                r = rstd[:, at:at + width]
                pool.tensor_tensor(r, r, half[:, 0:1].broadcast_to([P, width]), ALU.pow).then_inc(rstd_ready, 1)

            def token_roots():
                for t in range(TT):
                    inverse_roots(t, 1)

            for n in range(HALF):
                f = float(np.float32(10000.0) ** np.float32(-n / HALF))
                pool.memset(inv_freq[:, n:n + 1], f).then_inc(const, 1)
            token_roots()
            for n in (1, 2):
                split_lo(pool, mla_use(n), IN_TILES[n][1] * LAT)
            pool.wait_ge(xn_ready, TT)
            pool.dma_start(gain_mla[:, 0:QR], mla_q_norm[0].partition_broadcast(P)).then_inc(gain_in[1], 16)
            pool.dma_start(gain_mla[:, QR:QR + KVR], mla_kv_norm[0].partition_broadcast(P)).then_inc(gain_lat, 16)
            for n in range(W_UQ, W_UKV):
                split_lo(pool, mla_use(n), UQ)
            pool.wait_ge(trig_ready, 1)

            def rope(t, src, dst, width, areas):
                sin = trig[:, 0, t].unsqueeze(1).broadcast_to([P, width, HALF])
                cos = trig[:, 1, t].unsqueeze(1).broadcast_to([P, width, HALF])
                x1, x2 = src[:, :, 0:HALF], src[:, :, HALF:ROPE]
                a, b, c = areas
                pool.tensor_tensor(a, x1, cos, ALU.mult).then_inc(pool_link, 1)
                pool.tensor_tensor(b, x2, sin, ALU.mult).then_inc(pool_link, 1)
                links[0] += 2
                link(pool.tensor_tensor(c, x1, sin, ALU.mult))
                link(pool.tensor_tensor(dst[:, :, 0:HALF], a, b, ALU.subtract))
                link(pool.tensor_tensor(a, x2, cos, ALU.mult))
                link(pool.tensor_tensor(dst[:, :, HALF:ROPE], a, c, ALU.add))

            def areas(t, width):
                return [k[:, t, 0:width, NOPE + 16 * 0:NOPE + 16], k[:, t, 0:width, NOPE + 16:NOPE + 32],
                        rope_area[:, 0:width, :]]

            for t in range(TT):
                inverse_roots(2 * t, 2)
            for t in range(TT):
                kr = latent[:, t, QR + KVR:LAT].unsqueeze(1)
                rope(t, kr, kr, 1, areas(t, 1))
            for t in range(TT):
                pool.wait_ge(q_copied, 3 * (t + 1))
                qr = q[:, t, :, NOPE:QK]
                rope(t, qr, qr, HEADS, areas(t, HEADS))
                pool.tensor_copy(k[:, t, :, NOPE:QK],
                                 latent[:, t, QR + KVR:LAT].unsqueeze(1).broadcast_to([P, HEADS, ROPE])
                                 ).then_inc(qk_ready, 1)
            pool.wait_ge(heads_over, 1)
            gain(2, gain_ffn[:], norm_ffn[0])
            token_roots()
            with pool.Fori(0, STEPS) as i:
                split_lo(pool, (SLOTS - 1, i + FFN_BASE + 1))
            pool.wait_ge(xn_ready, 2 * TT)
            gain(3, gain_lru[:, 0:D], norm_mix[1])
            pool.memset(x_br[:, :, 0:CONV - 1], 0.0).then_inc(pads, 1)
            token_roots()
            for n in [L_AX] + [L_G + i for i in range(4)] + [L_OUT + i for i in range(4)]:
                split_lo(pool, lru_use(n))
            split_lo(pool, (1, MOE_BASE[1] + 1))
            pool.wait_ge(yT_lo, 2)
            gain(4, gain_moe[:], norm_ffn[1])
            gain(5, gain_out[:], norm_final)
            pool.dma_start(wr[:], moe_w_router[0].rearrange("(k p) e -> p k e", p=P)).then_inc(wr_in, 16)
            pool.memset(ones[:], 1.0).then_inc(moe_const, 1)
            pool.memset(before[:], 1.0).then_inc(moe_const, 1)
            pool.wait_ge(moe_const, 2)
            pool.affine_select(out=before[:], in_=before[:], compare_op=ALU.is_gt, fill=0.0, base=0,
                               pattern=[[1, P]], channel_multiplier=-1).then_inc(moe_const, 1)
            pool.iota(slot_no[:], pattern=[[1, SLOT_TOKENS]], base=0, channel_multiplier=0,
                      allow_small_or_imprecise_dtypes=True).then_inc(moe_const, 1)
            pool.iota(expert_no[:], pattern=[[0, TT], [1, E]], base=0, channel_multiplier=0,
                      allow_small_or_imprecise_dtypes=True).then_inc(moe_const, 1)
            pool.memset(key[:], -1.0).then_inc(moe_const, 1)
            token_roots()
            pool.wait_ge(logit_ps, 1)
            for t in range(TT):
                pool.wait_ge(xnh_ready, t + 1)
                pool.tensor_tensor(xn_lo[:, t], xn_moe[:, t], xn_hi[:, t].bitcast(F32),
                                   ALU.subtract).then_inc(xn_lo_ready, 1)
            pool.wait_ge(plan_ready, 1)
            n_pass = pool.value_load(n_pass_i[0:1, 0:1], min_val=1, max_val=2)

            def pool_use(s, step):
                return s, step + (MOE_BASE[s] + 1)

            with pool.Fori(0, n_pass) as p:
                with pool.Fori(0, E * STEPS - 1) as j:
                    split_lo(pool, pool_use(5, p * (E * STEPS) + j))
                    split_lo(pool, pool_use(1, p * (E * STEPS) + j + 1))
                split_lo(pool, pool_use(5, p * (E * STEPS) + (E * STEPS - 1)))
                with pool.If(n_pass > p + 1):
                    split_lo(pool, pool_use(1, p * (E * STEPS) + E * STEPS))
            token_roots()

        @block.scalar
        def _(act):
            def copy(dst, src):
                return act.activation(dst, src, ACT.Copy)

            for n in range(W_IN, W_UQ):
                split_hi(act, mla_use(n), IN_TILES[n][1] * LAT)
            xT_high(act, 0, xTh_mla)
            for n in range(W_UQ, W_UKV):
                split_hi(act, mla_use(n), UQ)
            act.wait_ge(angles, 1)
            act.activation(trig[:], red[:], ACT.Sin).then_inc(trig_ready, 1)
            for t in range(TT):
                for b, (c0, c1) in enumerate([(0, BANK), (BANK, LAT)]):
                    if t == TT - 1 and b == 1:
                        act.wait_ge(used[mla_use(W_UQ - 1)[0]], 1)
                    else:
                        act.wait_ge(lat_ps, 2 * t + b + 1)
                    copy(latent[:, t, c0:c1], psum[:, 4 + 2 * t + b, 0:c1 - c0]).then_inc(lat_ready, 1)
            for n in range(W_UKV, W_O):
                split_hi(act, mla_use(n), UKV)
            for t in range(TT):
                for b, n in enumerate([4, 1]):
                    act.wait_ge(c_ps, 2 * t + b + 1)
                    copy(c_hi[:, 4 * b:4 * b + n, t * P:(t + 1) * P],
                         psum[:, 2 * t + b, 0:n * P].rearrange("p (a b) -> p a b", b=P)).then_inc(c_hi_s, 1)
            for t in range(TT):
                for b in range(3):
                    if t == TT - 1 and b == 2:
                        act.wait_ge(used[mla_use(W_UKV - 1)[0]], mla_use(W_UKV - 1)[1])
                    else:
                        act.wait_ge(q_ps, 3 * t + b + 1)
                    copy(q[:, t].rearrange("p h c -> p (h c)")[:, b * BANK:(b + 1) * BANK],
                         psum[:, Q_BANKS[t][b]]).then_inc(q_copied, 1)
            for n in range(W_O, W_O + 2):
                split_hi(act, mla_use(n))
            for t in range(TT):
                for b in (0, 1):
                    act.wait_ge(kv_ps, 4 * t + b + 1)
                    src = psum[:, KV_BANKS[t][b]].rearrange("p (h c) -> p h c", h=4)
                    copy(k[:, t, 4 * b:4 * b + 4, 0:NOPE], src[:, :, 0:NOPE]).then_inc(kv_copied_a, 1)
                    copy(v[:, t, 4 * b * V:4 * (b + 1) * V].rearrange("p (h c) -> p h c", h=4),
                         src[:, :, NOPE:NOPE + V]).then_inc(kv_copied_a, 1)
            for n in range(W_O + 2, W_O + 4):
                split_hi(act, mla_use(n))

            def qk_copy(h):
                act.wait_ge(qkT_ps, h + 1)
                copy(qkT[0:QK, h % 2, :], psum[0:QK, h % 2, :]).then_inc(qkT_ready, 1)

            def exps(h):
                act.wait_ge(max_ready, h + 1)
                b = h % 2
                for r, (c0, c1) in enumerate([(0, P), (P, 3 * P)]):
                    act.activation(probs[:, b, c0:c1], probs[:, b, c0:c1], ACT.Exp, scale=SCALE,
                                   bias=nmx[:, 2 * b + r:2 * b + r + 1],
                                   accum_out=tot[:, 2 * b + r:2 * b + r + 1]).then_inc(exp_ready, 1)

            def pT_copy(h):
                act.wait_ge(probsT_ps, h + 1)
                copy(probs_T[:, h % 2, :], psum[:, 4 + h % 2, 0:3 * P]).then_inc(probsT_ready, 1)

            def o_high(g):
                act.wait_ge(o_ps, g + 1)
                copy(xTh_mla[:, g, :], psum[:, 6 + g % 2, 0:T]).then_inc(o_hi, 1)

            for i in range(HEADS + 5):
                if 0 <= i - 2 < HEADS:
                    exps(i - 2)
                if 0 <= i - 3 < HEADS:
                    pT_copy(i - 3)
                if i < HEADS:
                    qk_copy(i)
                if i >= 6 and i % 2 == 0:
                    o_high((i - 6) // 2)

            for s in (0, 1):
                split_hi(act, (s, FFN_BASE + 1))
            act.wait_ge(sp_in, 1)
            act.activation(sp_t[:, 0], sp_t[:, 1], ACT.Exp, scale=-1.0).then_inc(sp_exp, 1)
            xT_high(act, 1, xTh_ffn)
            for s in (2, 3):
                split_hi(act, (s, FFN_BASE + 1))
            with act.Fori(0, STEPS) as i:
                split_hi(act, (4, i + FFN_BASE + 1))
                act.wait_ge(fg_ps, i + 1)
                act.activation(hid_f[:, 0], psum[:, 0], ACT.Tanh, scale=0.5).then_inc(f_tanh, 1)
                split_hi(act, (5, i + FFN_BASE + 1))
                act.wait_ge(used[1], i + FFN_BASE + 1)
                act.activation(hid_f[:, 1], psum[:, 2], ACT.Tanh, scale=0.5).then_inc(f_tanh, 1)
                for t in range(TT):
                    act.wait_ge(fT_ps, i * TT + t + 1)
                    copy(hTh_f[:, t], psum[:, 2 * t].rearrange("p (a b) -> p a b", b=P)).then_inc(fT_hi, 1)
                    for s in (2 * t, 2 * t + 1):
                        split_hi(act, (s, i + FFN_BASE + 2))

            s_ax = lru_use(L_AX)
            act.wait_ge(wx_landed, 16)
            split_hi(act, s_ax)
            xT_high(act, 2, xTh_lru)
            split_hi(act, lru_use(L_G))

            def x_copy(c):
                s, n = lru_use(L_X + c // 2)
                if c % 2 == 0:
                    act.wait_ge(xbr_ps, c // 2 + 1)
                else:
                    act.wait_ge(used[s], n)
                copy(x_br[:, c, CONV - 1:], psum[:, c % 2, 0:T]).then_inc(xbr_copied, 1)

            def xc_high(c):
                act.wait_ge(xc_ready, c + 1)
                if c > 1:
                    act.wait_ge(ri_ps, c - 1)
                copy(xch[:, c % 2], states[:, c]).then_inc(xc_hi, 1)

            def sigmoids(c):
                if c < KT - 1:
                    act.wait_ge(ri_ps, c + 1)
                else:
                    act.wait_ge(used[s_ax[0]], s_ax[1])
                for g, dst in enumerate([decay[:, c], drive[:, c]]):
                    act.activation(dst, psum[:, 2 + c % 2, g * T:(g + 1) * T], ACT.Sigmoid,
                                   bias=par[:, BA + g * KT + c:BA + g * KT + c + 1]).then_inc(ri_ready, 1)

            def gate_out(c, func):
                s, n = lru_use(L_G + c // 2)
                if c % 2 == 0:
                    act.wait_ge(gate_ps, c // 2 + 1)
                else:
                    act.wait_ge(used[s], n)
                act.activation(gate_br[:, c, :], psum[:, 4 + c % 4, 0:T], func).then_inc(gate_copied, 1)

            SPLITS = {2: L_G + 1, 4: L_G + 2, 6: L_G + 3, 8: L_OUT, 9: L_OUT + 1, 10: L_OUT + 2}
            for i in range(KT + 3):
                if i < KT:
                    x_copy(i)
                if 0 <= i - 1 < KT:
                    xc_high(i - 1)
                if 0 <= i - 3 < KT:
                    sigmoids(i - 3)
                if i in SPLITS:
                    split_hi(act, lru_use(SPLITS[i]))
            for h in range(2):
                s4 = slice(4 * h, 4 * h + 4)
                act.wait_ge(log_a, 4 * h + 4)
                act.activation(states[:, s4], decay[:, s4], ACT.Tanh, scale=-1.0).then_inc(a_ready, 1)
                act.activation(decay[:, s4], decay[:, s4], ACT.Exp).then_inc(a_ready, 1)
            for c in range(4):
                gate_out(c, ACT.Copy)
            for h in range(2):
                act.wait_ge(mult_in, 4 * h + 4)
                act.activation(states[:, 4 * h:4 * h + 4], states[:, 4 * h:4 * h + 4],
                               ACT.Sqrt).then_inc(mult_ready, 1)
            gate_out(4, ACT.Gelu_apprx_tanh)
            act.wait_ge(gate_copied, 4)
            act.activation(gate_br[:, 0:4], gate_br[:, 0:4], ACT.Gelu_apprx_tanh).then_inc(gelu_ready, 1)
            gate_out(5, ACT.Gelu_apprx_tanh)
            split_hi(act, lru_use(L_OUT + 3))
            gate_out(6, ACT.Gelu_apprx_tanh)
            gate_out(7, ACT.Gelu_apprx_tanh)
            act.wait_ge(y_ready, 1)
            copy(xTh_lru[:, 0:4, :], states[:, 0:4, :]).then_inc(yT_hi, 1)
            act.wait_ge(y_ready, 2)
            copy(xTh_lru[:, 4:8, :], states[:, 4:8, :]).then_inc(yT_hi, 1)
            for s in (1, 2):
                split_hi(act, (s, MOE_BASE[s] + 1))

            act.wait_ge(wr_in, 16)
            copy(wr_hi[:], wr[:]).then_inc(wr_hi_s, 1)
            split_hi(act, (0, MOE_BASE[0] + 1))
            xT_high(act, 3, xTh_moe)
            split_hi(act, (3, MOE_BASE[3] + 1))
            act.wait_ge(logit_ps, 1)
            copy(logits_T[:], psum[0:E, 4, 0:T]).then_inc(logit_copied, 1)
            for t in range(TT):
                copy(xn_hi[:, t], xn_moe[:, t]).then_inc(xnh_ready, 1)
            act.wait_ge(top_diff, 1)
            act.activation(rs[:, 3], rs[:, 2], ACT.Exp).then_inc(top_exp, 1)
            act.wait_ge(plan_ready, 1)
            n_pass = act.value_load(n_pass_i[0:1, 0:1], min_val=1, max_val=2)

            def xg_high(n):
                for b in range(2):
                    act.wait_ge(gather_ps, n * 2 + (b - 1))
                    copy(xg_hi[:, 4 * b:4 * b + 4, :],
                         psum[:, 6 + b].rearrange("p (a b) -> p a b", b=P)).then_inc(xg_hi_s, 1)

            def onehot_T_copy(n):
                act.wait_ge(ohT_ps, n)
                copy(onehot_T[:], psum[:, 1, 256:512].rearrange("p (a b) -> p a b", b=P)).then_inc(ohT_ready, 1)

            def use(s, step):
                return s, step + (MOE_BASE[s] + 1)

            def step_work(step, more=True, first=None, last=None):
                if first is not None:
                    act.wait_ge(used[5], use(5, step)[1] - 1)
                    for b in range(2):
                        copy(y_hi[:, b * BANK:(b + 1) * BANK], psum[:, 4 + b]).then_inc(y_hi_s, 1)
                split_hi(act, use(4, step))
                act.wait_ge(mg_ps, step + 1)
                act.activation(hid_m[:, 0:256], psum[:, 0, 0:256], ACT.Tanh, scale=0.5).then_inc(m_tanh, 1)
                split_hi(act, use(5, step))
                act.wait_ge(used[1], use(1, step)[1])
                act.activation(hid_m[:, 256:512], psum[:, 2, 0:256], ACT.Tanh, scale=0.5).then_inc(m_tanh, 1)
                for b in range(2):
                    if b == 1 and more:
                        for s in (0, 1, 2) if last is not None else (0, 1):
                            split_hi(act, use(s, step + 1))
                    act.wait_ge(mT_ps, step * 2 + (b + 1))
                    copy(hTh_m[:, 2 * b:2 * b + 2],
                         psum[:, 2 * b, 256:512].rearrange("p (a b) -> p a b", b=P)).then_inc(mT_hi, 1)
                if last is not None:
                    xg_high(last + 2)
                if first is not None:
                    act.wait_ge(comb_ps, first * 4 + 4)
                    onehot_T_copy(first + 2)
                if more:
                    for s in (3,) if last is not None else (2, 3):
                        split_hi(act, use(s, step + 1))

            def expert_work(p, e, more):
                step, count = p * (E * STEPS) + e * STEPS, p * (E + 1) + e
                step_work(step, first=count)
                with act.Fori(1, STEPS - 1) as j:
                    step_work(step + j)
                step_work(step + (STEPS - 1), more=more, last=count)

            with act.Fori(0, n_pass) as p:
                xg_high(p * (E + 1) + 1)
                onehot_T_copy(p * (E + 1) + 1)
                with act.Fori(0, E - 1) as e:
                    expert_work(p, e, True)
                expert_work(p, E - 1, False)
                act.wait_ge(used[5], use(5, p * (E * STEPS))[1] + (E * STEPS - 1))
                for b in range(2):
                    copy(y_hi[:, b * BANK:(b + 1) * BANK], psum[:, 4 + b]).then_inc(y_hi_s, 1)
                with act.If(n_pass > p + 1):
                    for s in range(4):
                        split_hi(act, use(s, p * (E * STEPS) + E * STEPS))

        @block.tensor
        def _(pe):
            pe.wait_ge(const, 1)
            transpose_tokens(pe, 0, xn_mla)

            pe.wait_ge(xT_lo, 4)
            for t in range(TT):
                if t == 1:
                    pe.wait_ge(cols_ready, 1)
                    pe.transpose(psum[:, 0, 0:TT], pos_f, ident[0:TT, 0:TT]).then_inc(rows_ps, 1)
                    pe.transpose(psum[:, 1, 0:64], rows[0:64, :], ident[0:64, 0:64]).then_inc(rows_ps, 1)
                for b, (c0, c1) in enumerate([(0, BANK), (BANK, LAT)]):
                    terms, marks, units = [], {}, {}
                    last = t == TT - 1 and b == 1
                    for n, (k0, nk) in enumerate(IN_TILES):
                        if t == 0 and b == 0:
                            units[k0] = mla_use(n)
                        s = mla_use(n)[0]
                        for a in range(nk):
                            tok = slice(t * P, (t + 1) * P)
                            terms.append((xTh_mla[:, k0 + a, tok], xTl_mla[:, k0 + a, tok],
                                          unit(w_hi, s, LAT)[:, a, c0:c1], unit(w_lo, s, LAT)[:, a, c0:c1]))
                        if last:
                            marks[len(terms) - 1] = used[s]
                    if not last:
                        marks[len(terms) - 1] = lat_ps
                    product(pe, psum[:, 4 + 2 * t + b, 0:c1 - c0], terms, marks=marks, units=units)
            pe.wait_ge(cols_ready, 3)
            for t in range(TT):
                pe.wait_ge(c_ready, 2 * (t + 1))
                for b, n in enumerate([4, 1]):
                    for a in range(n):
                        col = (4 * b + a) * P
                        mm = pe.transpose(psum[:, 2 * t + b, a * P:(a + 1) * P],
                                          latent[:, t, col:col + P], ident[:])
                    mm.then_inc(c_ps, 1)

            def up_projection(first, tiles, k0, banks, done):
                for t in range(TT):
                    pe.wait_ge(c_lo_s, 2 * (t + 1))
                    for b, bank in enumerate(banks[t]):
                        terms, marks, units = [], {}, {}
                        last = t == TT - 1 and b == len(banks[t]) - 1
                        for a in range(tiles):
                            s = mla_use(first + a)[0]
                            if t == 0 and b == 0:
                                units[a] = mla_use(first + a)
                            tok = slice(t * P, (t + 1) * P)
                            cols = slice(b * BANK, (b + 1) * BANK)
                            terms.append((c_hi[:, k0 + a, tok], c_lo[:, k0 + a, tok], w_hi[:, s, cols], w_lo[:, s, cols]))
                            if last:
                                marks[a] = used[s]
                        if not last:
                            marks[tiles - 1] = done
                        for sm, n in BANK_FREE.get((first, t, b), ()):
                            pe.wait_ge(sm, n)
                        product(pe, psum[:, bank], terms, marks=marks, units=units)

            BANK_FREE = {
                (W_UQ, 0, 0): [(lat_ready, 4)],
                (W_UQ, 1, 0): [(c_lo_s, 4)],
                (W_UKV, 0, 2): [(q_copied, 1)], (W_UKV, 0, 3): [(q_copied, 2)],
                (W_UKV, 1, 0): [(q_copied, 3)], (W_UKV, 1, 1): [(q_copied, 4)],
                (W_UKV, 1, 2): [(q_copied, 5)], (W_UKV, 1, 3): [(q_copied, 6)],
            }
            up_projection(W_UQ, QR // P, 0, Q_BANKS, q_ps)
            up_projection(W_UKV, KVR // P, QR // P, KV_BANKS, kv_ps)

            def transpose_qk(h):
                if h >= 2:
                    pe.wait_ge(qkT_ready, h - 1)
                for n, src in enumerate([q[:, 0, h], q[:, 1, h], k[:, 0, h], k[:, 1, h]]):
                    mm = pe.transpose(psum[0:QK, h % 2, n * P:(n + 1) * P], src, ident[:])
                mm.then_inc(qkT_ps, 1)

            def scores(h):
                pe.wait_ge(qkT_ready, h + 1)
                if h >= 2:
                    pe.wait_ge(max_ready, h - 1)
                s = qkT[0:QK, h % 2]
                pe.matmul(psum[:, 2 + h % 2, 0:P], s[:, 0:P], s[:, 2 * P:3 * P], start=True, stop=True)
                pe.matmul(psum[:, 2 + h % 2, P:3 * P], s[:, P:2 * P], s[:, 2 * P:4 * P],
                          start=True, stop=True).then_inc(score_ps, 1)

            def transpose_probs(h):
                pe.wait_ge(probs_ready, h + 1)
                if h >= 2:
                    pe.wait_ge(probsT_ready, h - 1)
                for n in range(3):
                    mm = pe.transpose(psum[:, 4 + h % 2, n * P:(n + 1) * P],
                                      probs[:, h % 2, n * P:(n + 1) * P], ident[:])
                mm.then_inc(probsT_ps, 1)

            def values(h):
                g, r = h // 2, (h % 2) * V
                pe.wait_ge(probsT_ready, h + 1)
                if h % 2 == 0 and g >= 2:
                    pe.wait_ge(o_lo, g - 1)
                p_ = probs_T[:, h % 2]
                pe.matmul(psum[r:r + V, 6 + g % 2, 0:T], v[:, 0, h * V:(h + 1) * V], p_[:, 0:T],
                          start=True, stop=False)
                mm = pe.matmul(psum[r:r + V, 6 + g % 2, P:T], v[:, 1, h * V:(h + 1) * V], p_[:, T:3 * P],
                               start=False, stop=True)
                if h % 2 == 1:
                    mm.then_inc(o_ps, 1)

            pe.wait_ge(qk_ready, TT)
            pe.wait_ge(kv_copied_a, 4 * TT)
            pe.wait_ge(kv_copied_v, 4 * TT)
            for i in range(HEADS + 4):
                if 0 <= i - 3 < HEADS:
                    transpose_probs(i - 3)
                if 0 <= i - 4:
                    values(i - 4)
                if 0 <= i - 1 < HEADS:
                    scores(i - 1)
                if i < HEADS:
                    transpose_qk(i)

            def out_projection(use, first, hT, lT, done, rest=None):
                for t in range(TT):
                    for b in range(2):
                        terms, marks, units = [], {}, {}
                        last = t == TT - 1 and b == 1
                        for a in range(KT):
                            s = use(first + a // 2)[0]
                            if t == 0 and b == 0 and a % 2 == 0:
                                units[a] = use(first + a // 2)
                            tok, cols = slice(t * P, (t + 1) * P), slice(b * BANK, (b + 1) * BANK)
                            terms.append((hT[:, a, tok], lT[:, a, tok], unit(w_hi, s, D)[:, a % 2, cols],
                                          unit(w_lo, s, D)[:, a % 2, cols]))
                            if last and a % 2 == 1:
                                marks[a] = used[s]
                        if not last:
                            marks[KT - 1] = done
                        if t == 0 and b == 0 and rest is not None:
                            product(pe, psum[:, 0], terms[0:4], stop=False, units={0: units[0], 2: units[2]})
                            pe.wait_ge(*rest)
                            product(pe, psum[:, 0], terms[4:8], start=False, marks={3: done},
                                    units={0: units[4], 2: units[6]})
                        else:
                            product(pe, psum[:, 2 * t + b], terms, marks=marks, units=units)

            pe.wait_ge(o_lo, HEADS // 2)
            pe.wait_ge(probsT_ready, HEADS)
            out_projection(mla_use, W_O, xTh_mla, xTl_mla, proj_ps)

            transpose_tokens(pe, 1, xn_ffn)
            pe.wait_ge(xT_lo, 8)
            for b in range(4):
                pe.matmul(psum[:, 4 + b, 0:P], zeros[:], zeros[:], start=True, stop=False, skip_group_check=True)
            with pe.Fori(0, STEPS) as i:
                def half_layer(w, t, bank, marks):
                    units = {4 * h: (2 * w + h, i + FFN_BASE + 1) for h in range(2)} if t == 0 else {}
                    tok = slice(t * P, (t + 1) * P)
                    product(pe, psum[:, bank], [
                        (xTh_ffn[:, a, tok], xTl_ffn[:, a, tok], unit(w_hi, 2 * w + a // 4, BANK)[:, a % 4],
                         unit(w_lo, 2 * w + a // 4, BANK)[:, a % 4]) for a in range(KT)], marks=marks, units=units)

                def transpose_hidden(t):
                    pe.wait_ge(f_hid, i * TT + (t + 1))
                    for a in range(4):
                        mm = pe.transpose(psum[:, 2 * t, a * P:(a + 1) * P], hid_f[:, t, a * P:(a + 1) * P], ident[:])
                    mm.then_inc(fT_ps, 1)

                def down(t, b, marks):
                    units = {2 * h: (4 + h, i + FFN_BASE + 1) for h in range(2)} if t == 0 and b == 0 else {}
                    product(pe, psum[:, 4 + 2 * t + b], [
                        (hTh_f[:, t, a], hTl_f[:, t, a],
                         unit(w_hi, 4 + a // 2, D)[:, a % 2, b * BANK:(b + 1) * BANK],
                         unit(w_lo, 4 + a // 2, D)[:, a % 2, b * BANK:(b + 1) * BANK]) for a in range(4)],
                        start=False, stop=False, marks=marks, units=units)

                half_layer(0, 0, 0, {KT - 1: fg_ps})
                half_layer(1, 0, 1, {KT - 1: fu_ps})
                half_layer(0, 1, 2, {3: used[0], 7: used[1]})
                transpose_hidden(0)
                half_layer(1, 1, 3, {3: used[2], 7: used[3]})
                pe.wait_ge(fT_lo, i * TT + 1)
                down(0, 0, {})
                transpose_hidden(1)
                down(0, 1, {3: fd_ps})
                pe.wait_ge(fT_lo, i * TT + 2)
                down(1, 0, {})
                down(1, 1, {1: used[4], 3: used[5]})

            transpose_tokens(pe, 2, xn_lru)
            pe.wait_ge(xT_lo, 12)

            def channels(first, c, bank, done):
                s, n = lru_use(first + c // 2)
                if c % 2 == 0:
                    ready(pe, (s, n))
                cols = slice((c % 2) * P, (c % 2 + 1) * P)
                product(pe, psum[:, bank, 0:T], [
                    (unit(w_hi, s, 256)[:, a, cols], unit(w_lo, s, 256)[:, a, cols], xTh_lru[:, a], xTl_lru[:, a])
                    for a in range(KT)], marks={KT - 1: done if c % 2 == 0 else used[s]})

            def gates_of(c):
                s, n = lru_use(L_AX)
                if c == 0:
                    ready(pe, (s, n))
                if c >= 2:
                    pe.wait_ge(ri_ready, 2 * c - 2)
                pe.wait_ge(xc_lo, c + 1)
                for g in range(2):
                    wg_hi = unit(w_hi, s, P)[:, g * KT + c]
                    wg_lo = unit(w_lo, s, P)[:, g * KT + c]
                    product(pe, psum[:, 2 + c % 2, g * T:(g + 1) * T],
                            [(wg_hi, wg_lo, xch[:, c % 2], xcl[:, c % 2])],
                            marks={} if g == 0 else {0: ri_ps if c < KT - 1 else used[s]})

            for i in range(KT + 2):
                if i < KT:
                    if i >= 2:
                        pe.wait_ge(xbr_copied, i - 1)
                    channels(L_X, i, i % 2, xbr_ps)
                if i >= 2:
                    gates_of(i - 2)
            for c in range(KT):
                if c >= 4:
                    pe.wait_ge(gate_copied, c - 3)
                channels(L_G, c, 4 + c % 4, gate_ps)
            pe.wait_ge(yT_lo, 1)
            pe.wait_ge(ri_ready, 2 * KT)
            out_projection(lru_use, L_OUT, xTh_lru, xTl_lru, out_ps, rest=(yT_lo, 2))

            transpose_tokens(pe, 3, xn_moe)
            pe.wait_ge(xT_lo, 16)
            pe.wait_ge(wr_lo_s, 1)
            product(pe, psum[0:E, 4, 0:T], [(wr_hi[:, a], wr_lo[:, a], xTh_moe[:, a], xTl_moe[:, a])
                                            for a in range(KT)], marks={KT - 1: logit_ps})
            pe.wait_ge(logit_copied, 1)
            for t in range(TT):
                mm = pe.transpose(psum[:, 5, t * E:(t + 1) * E], logits_T[:, t * P:(t + 1) * P], ident[0:E, 0:E])
            mm.then_inc(logit_ps, 1)
            pe.wait_ge(mask_ready, 1)
            pe.wait_ge(moe_const, 6)
            sel = rt[:, 6]
            pe.matmul(psum[:, 6, 0:E], before[:], sel[:, 0], start=True, stop=True)
            pe.matmul(psum[:, 6, E:2 * E], before[:], sel[:, 1], start=True, stop=False)
            pe.matmul(psum[:, 6, E:2 * E], ones[:], sel[:, 0], start=False, stop=True)
            pe.matmul(psum[:, 6, 2 * E:3 * E], ones[:], sel[:, 0], start=True, stop=False)
            pe.matmul(psum[:, 6, 2 * E:3 * E], ones[:], sel[:, 1], start=False, stop=True).then_inc(rank_ps, 1)
            pe.wait_ge(plan_ready, 1)
            n_pass = pe.value_load(n_pass_i[0:1, 0:1], min_val=1, max_val=2)

            pe.wait_ge(xn_lo_ready, TT)

            def gather(n):
                pe.wait_ge(onehot_ready, n * 2)
                for b in range(2):
                    for a in range(4):
                        kt = 4 * b + a
                        for t in range(TT):
                            cols = slice(kt * P, (kt + 1) * P)
                            o = psum[:, 6 + b, a * P:(a + 1) * P]
                            pe.matmul(o, xn_hi[:, t, cols], onehot[:, t], start=t == 0, stop=False)
                            mm = pe.matmul(o, xn_lo[:, t, cols], onehot[:, t], start=False, stop=t == TT - 1)
                    mm.then_inc(gather_ps, 1)

            def transpose_onehot():
                for t in range(TT):
                    mm = pe.transpose(psum[:, 1, 256 + t * P:256 + (t + 1) * P], onehot[:, t].bitcast(F32), ident[:])
                mm.then_inc(ohT_ps, 1)

            def use(s, step):
                return s, step + (MOE_BASE[s] + 1)

            def expert_step(step, first=None, last=None):
                def half_layer(w, f, bank, marks):
                    units = {4 * h: use(2 * w + h, step) for h in range(2)} if f == 0 else {}
                    cols = slice(f * 256, (f + 1) * 256)
                    product(pe, psum[:, bank, 0:256], [
                        (xg_hi[:, a], xg_lo[:, a], unit(w_hi, 2 * w + a // 4, BANK)[:, a % 4, cols],
                         unit(w_lo, 2 * w + a // 4, BANK)[:, a % 4, cols]) for a in range(KT)], marks=marks,
                        units=units)

                def transpose_hidden(f):
                    pe.wait_ge(m_hid, step * 2 + (f + 1))
                    for a in range(2):
                        mm = pe.transpose(psum[:, 2 * f, 256 + a * P:256 + (a + 1) * P],
                                          hid_m[:, (2 * f + a) * P:(2 * f + a + 1) * P], ident[:])
                    mm.then_inc(mT_ps, 1)

                def down(f, b, marks):
                    product(pe, psum[:, 4 + b], [
                        (hTh_m[:, 2 * f + a], hTl_m[:, 2 * f + a],
                         unit(w_hi, 4 + f, D)[:, a, b * BANK:(b + 1) * BANK],
                         unit(w_lo, 4 + f, D)[:, a, b * BANK:(b + 1) * BANK]) for a in range(2)],
                        start=False, stop=False, marks=marks)

                half_layer(0, 0, 0, {KT - 1: mg_ps})
                half_layer(1, 0, 1, {KT - 1: mu_ps})
                if first is not None:
                    combine(first, 0)
                half_layer(0, 1, 2, {3: used[0], 7: used[1]})
                transpose_hidden(0)
                if first is not None:
                    transpose_onehot()
                half_layer(1, 1, 3, {3: used[2], 7: used[3]})
                if first is not None:
                    combine(first, 1)
                    for b in range(2):
                        pe.matmul(psum[:, 4 + b, 0:P], zeros[:], zeros[:], start=True, stop=False,
                                  skip_group_check=True)
                if last is not None:
                    pe.wait_ge(added, last * 4 + 5)
                    gather(last + 2)
                ready(pe, use(4, step))
                pe.wait_ge(mT_lo, step * 2 + 1)
                down(0, 0, {})
                transpose_hidden(1)
                down(0, 1, {1: used[4]})
                ready(pe, use(5, step))
                pe.wait_ge(mT_lo, step * 2 + 2)
                down(1, 0, {})
                down(1, 1, {1: used[5]})

            def combine(count, t):
                if t == 0:
                    pe.wait_ge(y_lo_s, count * 2 + 2)
                    pe.wait_ge(ohT_ready, count + 1)
                    pe.wait_ge(xg_lo_s, count * 2 + 2)
                else:
                    pe.wait_ge(added, count * 4 + 3)
                for b in range(2):
                    cols = slice(b * BANK, (b + 1) * BANK)
                    pe.matmul(psum[:, 6 + b], onehot_T[:, t], y_hi[:, cols], start=True, stop=False)
                    pe.matmul(psum[:, 6 + b], onehot_T[:, t], y_lo[:, cols], start=False,
                              stop=True).then_inc(comb_ps, 1)

            with pe.Fori(0, n_pass) as p:
                pe.wait_ge(added, p * (4 * (E + 1)) + 1)
                for b in range(2):
                    for a in range(4):
                        pe.matmul(psum[:, 4 + b, a * P:(a + 1) * P], zeros[:], zeros[:], start=True, stop=True)
                gather(p * (E + 1) + 1)
                transpose_onehot()
                with pe.Fori(0, E) as e:
                    count, step = p * (E + 1) + e, p * (E * STEPS) + e * STEPS
                    pe.wait_ge(xg_lo_s, count * 2 + 2)
                    pe.wait_ge(ohT_ready, count + 1)
                    expert_step(step, first=count)
                    with pe.Fori(1, STEPS - 1) as j:
                        expert_step(p * (E * STEPS) + e * STEPS + j)
                    expert_step(step + (STEPS - 1), last=count)
                for t in range(TT):
                    combine(p * (E + 1) + E, t)

        @block.vector
        def _(dve):
            links = [0]
            var_count = [0]

            def link(ins):
                links[0] += 1
                ins.then_inc(link_s, 1)
                dve.wait_ge(link_s, links[0])
                return ins

            def inverse_rms(n, src, scratch, width, at=0):
                for i in range(n):
                    link(dve.tensor_tensor_reduce(scratch[i], src[i], src[i], 1.0, 0.0, ALU.mult, ALU.add,
                                                  sumsq[:, at + i:at + i + 1]))
                s = slice(at, at + n)
                link(dve.tensor_scalar(rstd[:, s], sumsq[:, s], 1.0 / width, RMS_EPS, ALU.mult, ALU.add))
                dve.sem_inc(var_ready, 1)
                var_count[0] += 1
                dve.wait_ge(rstd_ready, var_count[0])

            def norm(t, xn, gain, arrived, done=xn_ready):
                inverse_rms(1, [res[:, t]], [xn[:, t]], D, at=t)
                dve.wait_ge(arrived, 16)
                dve.scalar_tensor_tensor(out=xn[:, t], in0=res[:, t], scalar=rstd[:, t:t + 1], in1=gain[:],
                                         op0=ALU.mult, op1=ALU.mult).then_inc(done, 1)

            def rope_angles():
                dve.wait_ge(small_in, 16 * 6)
                dve.tensor_copy(pos_f, pos_i).then_inc(cols_ready, 1)
                dve.wait_ge(rows_ps, 2)
                link(dve.tensor_copy(pos_col[:], psum[:, 0, 0:TT]))
                dve.sem_inc(cols_ready, 1)
                dve.tensor_copy(par[:], psum[:, 1, 0:64]).then_inc(cols_ready, 1)
                dve.wait_ge(const, 3 + HALF)
                for t in range(TT):
                    link(dve.tensor_scalar(ang[:, t], inv_freq[:], pos_col[:, t:t + 1], None, ALU.mult))
                two_pi = 2.0 * np.pi
                c1 = 6.28125
                c2 = float(np.floor((two_pi - c1) * 2.0 ** 21) / 2.0 ** 21)
                c3 = float(two_pi - c1 - c2)
                for n, shift in enumerate([0.0, 0.25]):
                    tn = turns[:, n]
                    link(dve.tensor_scalar(tn, ang[:], 1.0 / two_pi, shift, ALU.mult, ALU.add))
                    link(dve.tensor_scalar(tn, tn, ROUND, None, ALU.add))
                    link(dve.tensor_scalar(tn, tn, -ROUND, None, ALU.add))
                    src = ang[:]
                    for c in (c1, c2, c3):
                        link(dve.scalar_tensor_tensor(out=red[:, n], in0=tn, scalar=-c, in1=src,
                                                      op0=ALU.mult, op1=ALU.add))
                        src = red[:, n]
                link(dve.tensor_scalar(red[:, 1], red[:, 1], float(np.pi / 2), None, ALU.add))
                pi = float(np.nextafter(np.float32(np.pi), np.float32(0)))
                dve.tensor_scalar(red[:], red[:], pi, -pi, ALU.min, ALU.max).then_inc(angles, 1)

            for t in range(TT):
                dve.wait_ge(x_in[t], 16)
                norm(t, xn_mla, gain_mla, gain_in[0])
            split_lo(dve, mla_use(0), IN_TILES[0][1] * LAT)
            xT_low(dve, 0, xTl_mla, xTh_mla)
            rope_angles()
            parts = [(0, QR), (QR, QR + KVR)]
            for t in range(TT):
                dve.wait_ge(lat_ready, 2 * (t + 1))
                for n, (c0, c1) in enumerate(parts):
                    col = slice(2 * t + n, 2 * t + n + 1)
                    link(dve.tensor_tensor_reduce(v[:, t, c0:c1], latent[:, t, c0:c1], latent[:, t, c0:c1], 1.0,
                                                  0.0, ALU.mult, ALU.add, sumsq[:, col]))
                    link(dve.tensor_scalar(rstd[:, col], sumsq[:, col], 1.0 / (c1 - c0), RMS_EPS, ALU.mult,
                                           ALU.add))
                dve.sem_inc(var_ready, 1)
                var_count[0] += 1
                dve.wait_ge(rstd_ready, var_count[0])
                if t == 0:
                    dve.wait_ge(gain_in[1], 16)
                    dve.wait_ge(gain_lat, 16)
                for n, (c0, c1) in enumerate(parts):
                    dve.scalar_tensor_tensor(
                        out=latent[:, t, c0:c1], in0=latent[:, t, c0:c1],
                        scalar=rstd[:, 2 * t + n:2 * t + n + 1], in1=gain_mla[:, c0:c1],
                        op0=ALU.mult, op1=ALU.mult).then_inc(c_ready, 1)
            for t in range(TT):
                for b, n in enumerate([4, 1]):
                    dve.wait_ge(c_hi_s, 2 * t + b + 1)
                    area = (slice(None), slice(4 * b, 4 * b + n), slice(t * P, (t + 1) * P))
                    dve.tensor_tensor(c_lo[area], psum[:, 2 * t + b, 0:n * P].rearrange("p (a b) -> p a b", b=P),
                                      c_hi[area].bitcast(F32), ALU.subtract).then_inc(c_lo_s, 1)
            for n in range(W_UKV, W_O):
                split_lo(dve, mla_use(n), UKV)
            for n in range(W_O, W_O + 2):
                split_lo(dve, mla_use(n))
            for t in range(TT):
                for b in (2, 3):
                    if t == TT - 1 and b == 3:
                        dve.wait_ge(used[mla_use(W_O - 1)[0]], mla_use(W_O - 1)[1])
                    else:
                        dve.wait_ge(kv_ps, 4 * t + b + 1)
                    src = psum[:, KV_BANKS[t][b]].rearrange("p (h c) -> p h c", h=4)
                    dve.tensor_copy(k[:, t, 4 * b:4 * b + 4, 0:NOPE], src[:, :, 0:NOPE]).then_inc(kv_copied_v, 1)
                    dve.tensor_copy(v[:, t, 4 * b * V:4 * (b + 1) * V].rearrange("p (h c) -> p h c", h=4),
                                    src[:, :, NOPE:NOPE + V]).then_inc(kv_copied_v, 1)
            for n in range(W_O + 2, W_O + 4):
                split_lo(dve, mla_use(n))

            def maxima(h):
                b = h % 2
                dve.wait_ge(score_ps, h + 1)
                if h >= 2:
                    dve.wait_ge(probsT_ps, h - 1)
                for r, (c0, c1) in enumerate([(0, P), (P, 3 * P)]):
                    link(dve.tensor_tensor_reduce(probs[:, b, c0:c1], psum[:, 2 + b, c0:c1],
                                                  mask[:, 2 * P - (c1 - c0):2 * P], 1.0,
                                                  -BIG, ALU.add, ALU.max, mx[:, 2 * b + r:2 * b + r + 1]))
                dve.tensor_scalar(nmx[:, 2 * b:2 * b + 2], mx[:, 2 * b:2 * b + 2], -SCALE, None,
                                  ALU.mult).then_inc(max_ready, 1)

            def normalize(h):
                b = h % 2
                dve.wait_ge(exp_ready, 2 * h + 2)
                link(dve.reciprocal(inv[:, 2 * b:2 * b + 2], tot[:, 2 * b:2 * b + 2]))
                link(dve.tensor_scalar(probs[:, b, 0:P], probs[:, b, 0:P], inv[:, 2 * b:2 * b + 1], None, ALU.mult))
                dve.tensor_scalar(probs[:, b, P:3 * P], probs[:, b, P:3 * P], inv[:, 2 * b + 1:2 * b + 2], None,
                                  ALU.mult).then_inc(probs_ready, 1)

            def o_low(g):
                dve.wait_ge(o_hi, g + 1)
                dve.tensor_tensor(xTl_mla[:, g, :], psum[:, 6 + g % 2, 0:T], xTh_mla[:, g, :].bitcast(F32),
                                  ALU.subtract).then_inc(o_lo, 1)

            for i in range(HEADS + 5):
                if 0 <= i - 1 < HEADS:
                    maxima(i - 1)
                if 0 <= i - 2 < HEADS:
                    normalize(i - 2)
                if i >= 6 and i % 2 == 0:
                    o_low((i - 6) // 2)
            dve.wait_ge(o_ps, HEADS // 2)
            dve.sem_inc(heads_over, 1)

            def add_projection(t, done, last_use):
                for b in range(2):
                    if t == TT - 1 and b == 1:
                        dve.wait_ge(used[last_use[0]], last_use[1])
                    else:
                        dve.wait_ge(done, 2 * t + b + 1)
                    r = res[:, t, b * BANK:(b + 1) * BANK]
                    link(dve.tensor_tensor(r, r, psum[:, 2 * t + b], ALU.add))

            for s in (0, 1):
                split_lo(dve, (s, FFN_BASE + 1))
            dve.scalar_tensor_tensor(out=sp_t[:, 1], in0=par[:, LAM:LAM + KT], scalar=-1.0,
                                     in1=par[:, LAM:LAM + KT], op0=ALU.mult, op1=ALU.max).then_inc(sp_in, 1)
            link(dve.tensor_scalar(sp_t[:, 2], par[:, LAM:LAM + KT], -1.0, 0.0, ALU.mult, ALU.max))
            dve.wait_ge(sp_exp, 1)
            link(dve.tensor_scalar(sp_t[:, 3], sp_t[:, 0], 2.0, None, ALU.add))
            link(dve.reciprocal(sp_t[:, 3], sp_t[:, 3]))
            link(dve.tensor_tensor(sp_t[:, 3], sp_t[:, 0], sp_t[:, 3], ALU.mult))
            link(dve.tensor_tensor(sp_t[:, 4], sp_t[:, 3], sp_t[:, 3], ALU.mult))
            link(dve.memset(sp_t[:, 5], 0.0))
            for n in range(9, 0, -1):
                link(dve.scalar_tensor_tensor(out=sp_t[:, 5], in0=sp_t[:, 5], scalar=1.0 / (2 * n + 1),
                                              in1=sp_t[:, 4], op0=ALU.add, op1=ALU.mult))
            link(dve.scalar_tensor_tensor(out=sp_t[:, 5], in0=sp_t[:, 5], scalar=1.0, in1=sp_t[:, 3],
                                          op0=ALU.add, op1=ALU.mult))
            link(dve.scalar_tensor_tensor(out=sp_t[:, 6], in0=sp_t[:, 5], scalar=2.0, in1=sp_t[:, 2],
                                          op0=ALU.mult, op1=ALU.add))
            link(dve.tensor_scalar(sp_t[:, 7], sp_t[:, 6], -8.0, None, ALU.mult))
            dve.wait_ge(x_again, 16)
            for t in range(TT):
                add_projection(t, proj_ps, mla_use(W_O + 3))
                norm(t, xn_ffn, gain_ffn, gain_in[2])

            xT_low(dve, 1, xTl_ffn, xTh_ffn)
            for s in (2, 3):
                split_lo(dve, (s, FFN_BASE + 1))
            def f_silu(i, t):
                dve.wait_ge(f_tanh, i * TT + (t + 1))
                dve.scalar_tensor_tensor(out=hid_f[:, t], in0=hid_f[:, t], scalar=1.0, in1=psum[:, 2 * t],
                                         op0=ALU.add, op1=ALU.mult).then_inc(f_mid, 1)

            def f_times_up(i, t):
                dve.wait_ge(f_mid, i * TT + (t + 1))
                if t == 0:
                    dve.wait_ge(fu_ps, i + 1)
                else:
                    dve.wait_ge(used[3], i + FFN_BASE + 1)
                dve.scalar_tensor_tensor(out=hid_f[:, t], in0=hid_f[:, t], scalar=0.5, in1=psum[:, 2 * t + 1],
                                         op0=ALU.mult, op1=ALU.mult).then_inc(f_hid, 1)

            def f_hT_low(i, t):
                dve.wait_ge(fT_hi, i * TT + (t + 1))
                dve.tensor_tensor(hTl_f[:, t], psum[:, 2 * t].rearrange("p (a b) -> p a b", b=P),
                                  hTh_f[:, t].bitcast(F32), ALU.subtract).then_inc(fT_lo, 1)

            with dve.Fori(0, STEPS) as i:
                split_lo(dve, (4, i + FFN_BASE + 1))
                f_silu(i, 0)
                f_times_up(i, 0)
                f_silu(i, 1)
                f_hT_low(i, 0)
                split_lo(dve, (0, i + FFN_BASE + 2))
                f_times_up(i, 1)
                split_lo(dve, (1, i + FFN_BASE + 2))
                f_hT_low(i, 1)
                for s in (2, 3):
                    split_lo(dve, (s, i + FFN_BASE + 2))
            for t in range(TT):
                if t == 0:
                    dve.wait_ge(fd_ps, STEPS)
                else:
                    dve.wait_ge(used[5], FFN_BASE + STEPS)
                for b in range(2):
                    r = res[:, t, b * BANK:(b + 1) * BANK]
                    link(dve.tensor_tensor(r, r, psum[:, 4 + 2 * t + b], ALU.add))
                norm(t, xn_lru, gain_lru[:, 0:D], gain_in[3])

            xT_low(dve, 2, xTl_lru, xTh_lru)

            def conv(c):
                dve.wait_ge(xbr_copied, c + 1)
                if c == 0:
                    dve.wait_ge(pads, 1)
                link(dve.tensor_scalar(states[:, c], x_br[:, c, 0:T], par[:, c:c + 1], par[:, CB + c:CB + c + 1],
                                       ALU.mult, ALU.add))
                for w in range(1, CONV):
                    ins = dve.scalar_tensor_tensor(out=states[:, c], in0=x_br[:, c, w:w + T],
                                                   scalar=par[:, w * KT + c:w * KT + c + 1], in1=states[:, c],
                                                   op0=ALU.mult, op1=ALU.add)
                    if w < CONV - 1:
                        link(ins)
                ins.then_inc(xc_ready, 1)

            def xc_low(c):
                dve.wait_ge(xc_hi, c + 1)
                dve.tensor_tensor(xcl[:, c % 2], states[:, c], xch[:, c % 2].bitcast(F32),
                                  ALU.subtract).then_inc(xc_lo, 1)

            def drive_and_log(c):
                dve.wait_ge(ri_ready, 2 * c + 2)
                link(dve.tensor_tensor(drive[:, c], drive[:, c], states[:, c], ALU.mult))
                dve.tensor_scalar(decay[:, c], decay[:, c], sp_t[:, 7, c:c + 1], None,
                                  ALU.mult).then_inc(log_a, 1)

            for i in range(KT + 3):
                if i < KT:
                    conv(i)
                if 0 <= i - 1 < KT:
                    xc_low(i - 1)
                if 0 <= i - 3 < KT:
                    drive_and_log(i - 3)
            for c in range(KT):
                dve.wait_ge(a_ready, 2 * (c // 4 + 1))
                link(dve.tensor_tensor(a_sq[:], decay[:, c], decay[:, c], ALU.mult))
                dve.scalar_tensor_tensor(out=states[:, c], in0=a_sq[:], scalar=1.0, in1=states[:, c],
                                         op0=ALU.add, op1=ALU.mult).then_inc(mult_in, 1)
                dve.wait_ge(mult_in, c + 1)
            for h in range(2):
                s4 = slice(4 * h, 4 * h + 4)
                dve.wait_ge(mult_ready, h + 1)
                link(dve.tensor_tensor(drive[:, s4], drive[:, s4], states[:, s4], ALU.mult))
                for c in range(4 * h, 4 * h + 4):
                    dve.tensor_tensor_scan(states[:, c], decay[:, c], drive[:, c], 0.0, ALU.mult,
                                           ALU.add).then_inc(state_ready, 1)
            for h in range(2):
                s4 = slice(4 * h, 4 * h + 4)
                dve.wait_ge(state_ready, 4 * h + 4)
                if h == 0:
                    dve.wait_ge(gelu_ready, 1)
                else:
                    dve.wait_ge(gate_copied, KT)
                dve.tensor_tensor(states[:, s4], states[:, s4], gate_br[:, s4], ALU.mult).then_inc(y_ready, 1)
            for h in range(2):
                s4 = slice(4 * h, 4 * h + 4)
                dve.wait_ge(yT_hi, h + 1)
                dve.tensor_tensor(xTl_lru[:, s4], states[:, s4], xTh_lru[:, s4].bitcast(F32),
                                  ALU.subtract).then_inc(yT_lo, 1)
            split_lo(dve, (2, MOE_BASE[2] + 1))
            dve.wait_ge(wr_hi_s, 1)
            dve.tensor_tensor(wr_lo[:], wr[:], wr_hi[:].bitcast(F32), ALU.subtract).then_inc(wr_lo_s, 1)
            for t in range(TT):
                add_projection(t, out_ps, lru_use(L_OUT + 3))
                norm(t, xn_moe, gain_moe, gain_in[4])

            xT_low(dve, 3, xTl_moe, xTh_moe)
            for s in (0, 3):
                split_lo(dve, (s, MOE_BASE[s] + 1))
            dve.wait_ge(logit_ps, 2)
            lg = rt[:, 0]
            link(dve.tensor_copy(lg, psum[:, 5, 0:TT * E].rearrange("p (t e) -> p t e", e=E)))
            dve.wait_ge(moe_const, 6)

            def spread(a):
                return a.unsqueeze(2).broadcast_to([P, TT, E])

            def first_of_max(src, top, tmp, hot):
                link(dve.tensor_reduce(top, src, AX, ALU.max))
                link(dve.tensor_tensor(tmp, src, spread(top), ALU.is_equal))
                link(dve.scalar_tensor_tensor(out=tmp, in0=tmp, scalar=-64.0, in1=expert_no[:], op0=ALU.mult,
                                              op1=ALU.add))
                link(dve.tensor_reduce(rs[:, 7], tmp, AX, ALU.min))
                link(dve.tensor_tensor(hot, tmp, spread(rs[:, 7]), ALU.is_equal))

            first_of_max(lg, rs[:, 0], rt[:, 1], rt[:, 2])
            link(dve.scalar_tensor_tensor(out=rt[:, 3], in0=rt[:, 2], scalar=-BIG, in1=lg, op0=ALU.mult,
                                          op1=ALU.add))
            first_of_max(rt[:, 3], rs[:, 1], rt[:, 1], rt[:, 4])
            dve.tensor_tensor(rs[:, 2], rs[:, 1], rs[:, 0], ALU.subtract).then_inc(top_diff, 1)
            dve.tensor_tensor(rt[:, 6], rt[:, 2], rt[:, 4], ALU.add).then_inc(mask_ready, 1)
            dve.wait_ge(top_exp, 1)
            link(dve.tensor_scalar(rs[:, 4], rs[:, 3], 1.0, None, ALU.add))
            link(dve.reciprocal(rs[:, 4], rs[:, 4]))
            link(dve.tensor_tensor(rs[:, 5], rs[:, 3], rs[:, 4], ALU.mult))
            link(dve.tensor_tensor(rt[:, 5], rt[:, 2], spread(rs[:, 4]), ALU.mult))
            link(dve.tensor_tensor(rt[:, 7], rt[:, 4], spread(rs[:, 5]), ALU.mult))
            link(dve.memset(gates[:, :, 0:1], 0.0))
            link(dve.tensor_tensor(gates[:, :, 1:E + 1], rt[:, 5], rt[:, 7], ALU.add))
            dve.wait_ge(rank_ps, 1)
            ranks = psum[:, 6, 0:2 * E].rearrange("p (t e) -> p t e", e=E)
            link(dve.scalar_tensor_tensor(out=rt[:, 1], in0=ranks, scalar=1.0, in1=rt[:, 6], op0=ALU.add,
                                          op1=ALU.mult))
            link(dve.tensor_scalar(key[:, :, 0:E], rt[:, 1], -1.0, None, ALU.add))
            link(dve.tensor_reduce(rs[:, 6, 0:1], psum[:, 6, 2 * E:3 * E], AX, ALU.max))
            dve.tensor_scalar(n_pass_i[:], rs[0:1, 6, 0:1], float(SLOT_TOKENS), 1.0, ALU.is_gt,
                              ALU.add).then_inc(plan_ready, 1)
            dve.sem_inc(added, 1)
            dve.wait_ge(plan_ready, 1)
            n_pass = dve.value_load(n_pass_i[0:1, 0:1], min_val=1, max_val=2)

            def one_hot(e):
                for t in range(TT):
                    dve.tensor_scalar(onehot[:, t], slot_no[:], key[:, t, bass.ds(e, 1)], None,
                                      ALU.is_equal).then_inc(onehot_ready, 1)

            def xg_low(n):
                for b in range(2):
                    dve.wait_ge(xg_hi_s, n * 2 + (b - 1))
                    dve.tensor_tensor(xg_lo[:, 4 * b:4 * b + 4, :], psum[:, 6 + b].rearrange("p (a b) -> p a b", b=P),
                                      xg_hi[:, 4 * b:4 * b + 4, :].bitcast(F32), ALU.subtract).then_inc(xg_lo_s, 1)

            def use(s, step):
                return s, step + (MOE_BASE[s] + 1)

            def y_low(n):
                for b in range(2):
                    cols = slice(b * BANK, (b + 1) * BANK)
                    dve.wait_ge(y_hi_s, n * 2 + (b - 1))
                    dve.tensor_tensor(y_lo[:, cols], psum[:, 4 + b], y_hi[:, cols].bitcast(F32),
                                      ALU.subtract).then_inc(y_lo_s, 1)

            def add_results(count, e, t):
                for b in range(2):
                    dve.wait_ge(comb_ps, count * 4 + (2 * t + b + 1))
                    r = res[:, t, b * BANK:(b + 1) * BANK]
                    dve.scalar_tensor_tensor(out=r, in0=psum[:, 6 + b], scalar=gates[:, t, bass.ds(e, 1)],
                                             in1=r, op0=ALU.mult, op1=ALU.add).then_inc(added, 1)

            def step_work(step, more=True, first=None, last=None):
                def silu(f):
                    cols = slice(256 * f, 256 * (f + 1))
                    dve.wait_ge(m_tanh, step * 2 + (f + 1))
                    dve.scalar_tensor_tensor(out=hid_m[:, cols], in0=hid_m[:, cols], scalar=1.0,
                                             in1=psum[:, 2 * f, 0:256], op0=ALU.add, op1=ALU.mult).then_inc(m_mid, 1)

                def times_up(f):
                    cols = slice(256 * f, 256 * (f + 1))
                    dve.wait_ge(m_mid, step * 2 + (f + 1))
                    if f == 0:
                        dve.wait_ge(mu_ps, step + 1)
                    else:
                        dve.wait_ge(used[3], use(3, step)[1])
                    dve.scalar_tensor_tensor(out=hid_m[:, cols], in0=hid_m[:, cols], scalar=0.5,
                                             in1=psum[:, 2 * f + 1, 0:256], op0=ALU.mult,
                                             op1=ALU.mult).then_inc(m_hid, 1)

                def hT_low(f):
                    dve.wait_ge(mT_hi, step * 2 + (f + 1))
                    dve.tensor_tensor(hTl_m[:, 2 * f:2 * f + 2], psum[:, 2 * f, 256:512].rearrange("p (a b) -> p a b", b=P),
                                      hTh_m[:, 2 * f:2 * f + 2].bitcast(F32), ALU.subtract).then_inc(mT_lo, 1)

                if first is not None:
                    y_low(first[0] + 1)
                split_lo(dve, use(4, step))
                silu(0)
                times_up(0)
                silu(1)
                hT_low(0)
                if first is not None:
                    dve.wait_ge(added, first[0] * 4 + 1)
                    add_results(*first, 0)
                times_up(1)
                if more:
                    split_lo(dve, use(0, step + 1))
                hT_low(1)
                if last is not None:
                    xg_low(last[0] + 2)
                if more:
                    for s in (2, 3):
                        split_lo(dve, use(s, step + 1))
                if first is not None:
                    add_results(*first, 1)
                    dve.wait_ge(ohT_ps, first[0] + 2)
                    one_hot(first[1] + 1)

            def expert_work(p, e, more):
                step, count = p * (E * STEPS) + e * STEPS, p * (E + 1) + e
                step_work(step, first=(count, e))
                with dve.Fori(1, STEPS - 1) as j:
                    step_work(step + j)
                step_work(step + (STEPS - 1), more=more, last=(count, e))

            dve.sem_inc(pass_over, 1)
            with dve.Fori(0, n_pass) as p:
                dve.wait_ge(pass_over, p + 1)
                one_hot(0)
                xg_low(p * (E + 1) + 1)
                with dve.Fori(0, E - 1) as e:
                    expert_work(p, e, True)
                expert_work(p, E - 1, False)
                y_low(p * (E + 1) + (E + 1))
                dve.wait_ge(added, p * (4 * (E + 1)) + 4 * E + 1)
                for t in range(TT):
                    add_results(p * (E + 1) + E, E, t)
                dve.wait_ge(added, p * (4 * (E + 1)) + 4 * (E + 1) + 1)
                dve.tensor_scalar(key[:, :, 0:E], key[:, :, 0:E], float(-SLOT_TOKENS), None,
                                  ALU.add).then_inc(pass_over, 1)
                with dve.If(n_pass > p + 1):
                    for s in (0, 2, 3):
                        split_lo(dve, use(s, p * (E * STEPS) + E * STEPS))
            for t in range(TT):
                norm(t, xn_out, gain_out, gain_in[5], out_ready)


_INS = ["x", "positions", "norm_mix", "norm_ffn", "norm_final", "mla_w_in", "mla_q_norm", "mla_kv_norm",
        "mla_w_uq", "mla_w_ukv", "mla_w_o", "lru_w_in", "lru_conv_w", "lru_conv_b", "lru_w_a", "lru_b_a",
        "lru_w_x", "lru_b_x", "lru_lam", "lru_w_out", "ffn_w_gate", "ffn_w_up", "ffn_w_down", "moe_w_router",
        "moe_w_gate", "moe_w_up", "moe_w_down"]


def kernel(**inputs):
    import numpy as _np
    import concourse.bacc as _bacc
    from concourse import mybir as _mybir
    from concourse.bass_utils import run_bass_kernel_spmd as _run

    nc = _bacc.Bacc("TRN2", target_bir_lowering=False, num_devices=1)
    arrays, args = {}, []
    for name in _INS:
        a = _np.ascontiguousarray(inputs[name])
        arrays[f"in_{name}"] = a
        args.append(nc.dram_tensor(f"in_{name}", a.shape, _mybir.dt.from_np(a.dtype), kind="ExternalInput").ap())
    out = nc.dram_tensor("out", inputs["x"].shape, _mybir.dt.float32, kind="ExternalOutput").ap()
    trunk(nc, *args, out)
    r = _run(nc, [arrays], core_ids=[0])
    return r.results[0]["out"]
```
